# Optimizing a Trainium2 kernel written in Bass

```python
import math
import jax, jax.numpy as jnp
from jax import lax
import numpy as np

D_MODEL = 1024
BATCH = 1
SEQ = 1024
DEPTH = 1

MEM_LEN = 256
MLA_HEADS = 8
QK_NOPE_DIM = 64
QK_ROPE_DIM = 32
V_HEAD_DIM = 64
Q_LORA_RANK = 384
KV_LORA_RANK = 256
MLA_OUT = MLA_HEADS * V_HEAD_DIM
CONV_GROUPS = 8
CONV_DIM = 512
CONV_WIDTH = 3
GROUP_DIM = 64
MIX_WIDTH = MLA_OUT + CONV_DIM
IN_PROJ_COLS = Q_LORA_RANK + KV_LORA_RANK + QK_ROPE_DIM + 3 * CONV_DIM
ROPE_THETA = 10000.0
Q_BLOCK = 128
X_HEADS = 4
X_HEAD_DIM = D_MODEL // X_HEADS
PEER_HEADS = 8
PEER_KEYS = 128
PEER_EXPERTS = PEER_KEYS * PEER_KEYS
PEER_QDIM = 128
PEER_TOPK = 16
PEER_BLOCK = 128
EPS = 1e-6

kernel_name = 'hybrid_mla_shortconv_memxattn_peer'

def rmsnorm(t, g):
    tf = t.astype(jnp.float32)
    tf = tf * lax.rsqrt(jnp.mean(tf * tf, axis=-1, keepdims=True) + EPS)
    return (tf * g.astype(jnp.float32)).astype(t.dtype)

def rope_tables(positions, dim, dtype):
    inv = ROPE_THETA ** (-jnp.arange(0, dim, 2, dtype=jnp.float32) / dim)
    ang = positions.astype(jnp.float32)[..., None] * inv
    return jnp.cos(ang).astype(dtype), jnp.sin(ang).astype(dtype)

def apply_rope(t, cos, sin):
    half = t.shape[-1] // 2
    t1, t2 = t[..., :half], t[..., half:]
    return jnp.concatenate([t1 * cos - t2 * sin, t2 * cos + t1 * sin], axis=-1)

def mla_branch(c_q, c_kv, k_rope_raw, cos, sin, g_q, w_uq, g_kv, w_ukv):
    B, S, _ = c_q.shape
    q = (rmsnorm(c_q, g_q) @ w_uq).reshape(B, S, MLA_HEADS, QK_NOPE_DIM + QK_ROPE_DIM)
    q_nope = q[..., :QK_NOPE_DIM]
    q_rope = apply_rope(q[..., QK_NOPE_DIM:], cos[:, :, None, :], sin[:, :, None, :])
    kv = (rmsnorm(c_kv, g_kv) @ w_ukv).reshape(B, S, MLA_HEADS, QK_NOPE_DIM + V_HEAD_DIM)
    k_nope = kv[..., :QK_NOPE_DIM]
    v = kv[..., QK_NOPE_DIM:]
    k_rope = apply_rope(k_rope_raw, cos, sin)
    scale = 1.0 / math.sqrt(QK_NOPE_DIM + QK_ROPE_DIM)
    kpos = jnp.arange(S)

    def block(i):
        start = i * Q_BLOCK
        qn = lax.dynamic_slice_in_dim(q_nope, start, Q_BLOCK, axis=1)
        qr = lax.dynamic_slice_in_dim(q_rope, start, Q_BLOCK, axis=1)
        s = (jnp.einsum('bqhd,bkhd->bhqk', qn, k_nope)
             + jnp.einsum('bqhd,bkd->bhqk', qr, k_rope)).astype(jnp.float32) * scale
        qpos = start + jnp.arange(Q_BLOCK)
        mask = kpos[None, :] <= qpos[:, None]
        s = jnp.where(mask[None, None], s, -jnp.inf)
        p = jax.nn.softmax(s, axis=-1).astype(v.dtype)
        return jnp.einsum('bhqk,bkhd->bqhd', p, v)

    o = lax.map(block, jnp.arange(S // Q_BLOCK))
    return jnp.transpose(o, (1, 0, 2, 3, 4)).reshape(B, S, MLA_OUT)

def short_conv_branch(gate_b, gate_c, hx, conv_w):
    z = gate_c * hx
    zc = lax.conv_general_dilated(
        z, conv_w[:, None, :].astype(z.dtype), window_strides=(1,),
        padding=[(CONV_WIDTH - 1, 0)], dimension_numbers=('NWC', 'WIO', 'NWC'),
        feature_group_count=CONV_DIM)
    return gate_b * zc

def mixer_block(xn, cos, sin, w_in, g_q, w_uq, g_kv, w_ukv, conv_w, g_out, w_o):
    B, S, _ = xn.shape
    proj = xn @ w_in
    o1 = Q_LORA_RANK
    o2 = o1 + KV_LORA_RANK
    o3 = o2 + QK_ROPE_DIM
    o4 = o3 + CONV_DIM
    o5 = o4 + CONV_DIM
    y_mla = mla_branch(proj[..., :o1], proj[..., o1:o2], proj[..., o2:o3],
                       cos, sin, g_q, w_uq, g_kv, w_ukv)
    y_conv = short_conv_branch(proj[..., o3:o4], proj[..., o4:o5], proj[..., o5:], conv_w)
    y = jnp.concatenate([y_mla, y_conv], axis=-1).reshape(B, S, MIX_WIDTH // GROUP_DIM, GROUP_DIM)
    y = rmsnorm(y, g_out.reshape(MIX_WIDTH // GROUP_DIM, GROUP_DIM)).reshape(B, S, MIX_WIDTH)
    return y @ w_o

def memory_xattn(hn, memn, w_xq, w_xkv, w_xo):
    B, S, D = hn.shape
    M = memn.shape[1]
    q = (hn @ w_xq).reshape(B, S, X_HEADS, X_HEAD_DIM)
    kv = (memn @ w_xkv).reshape(B, M, 2, X_HEADS, X_HEAD_DIM)
    k, v = kv[:, :, 0], kv[:, :, 1]
    s = jnp.einsum('bshd,bmhd->bhsm', q, k).astype(jnp.float32) / math.sqrt(X_HEAD_DIM)
    p = jax.nn.softmax(s, axis=-1).astype(v.dtype)
    o = jnp.einsum('bhsm,bmhd->bshd', p, v).reshape(B, S, D)
    return o @ w_xo

def peer_ffn(hn, w_pq, sub_keys, u_experts, v_experts):
    B, S, D = hn.shape
    T = B * S
    xt = hn.reshape(T, D)
    q = (xt @ w_pq).reshape(T, PEER_HEADS, 2, PEER_QDIM // 2)
    s = jnp.einsum('thcd,hcnd->thcn', q, sub_keys).astype(jnp.float32)
    s_top, i_top = lax.top_k(s, PEER_TOPK)
    cand_s = (s_top[:, :, 0, :, None] + s_top[:, :, 1, None, :]).reshape(T, PEER_HEADS, PEER_TOPK * PEER_TOPK)
    cand_i = (i_top[:, :, 0, :, None] * PEER_KEYS + i_top[:, :, 1, None, :]).reshape(T, PEER_HEADS, PEER_TOPK * PEER_TOPK)
    best_s, best_pos = lax.top_k(cand_s, PEER_TOPK)
    experts = jnp.take_along_axis(cand_i, best_pos, axis=-1)
    gates = jax.nn.softmax(best_s, axis=-1).astype(hn.dtype)
    nb = T // PEER_BLOCK

    def block(args):
        xb, eb, gb = args
        u_sel = jnp.take(u_experts, eb, axis=0)
        a = jax.nn.gelu(jnp.einsum('td,thkd->thk', xb, u_sel)) * gb
        v_sel = jnp.take(v_experts, eb, axis=0)
        return jnp.einsum('thk,thkd->td', a, v_sel)

    out = lax.map(block, (xt.reshape(nb, PEER_BLOCK, D),
                          experts.reshape(nb, PEER_BLOCK, PEER_HEADS, PEER_TOPK),
                          gates.reshape(nb, PEER_BLOCK, PEER_HEADS, PEER_TOPK)))
    return out.reshape(B, S, D)

def setup_inputs(seed: int = 0) -> dict:
    key = jax.random.key(seed)
    ks = iter(jax.random.split(key, 32))
    f32 = jnp.float32

    def nrm(shape, scale):
        return jax.random.normal(next(ks), shape, f32) * scale

    def gain(shape):
        return 1.0 + 0.02 * jax.random.normal(next(ks), shape, f32)

    L = DEPTH
    x = jax.random.normal(next(ks), (BATCH, SEQ, D_MODEL), f32)
    mem = jax.random.normal(next(ks), (BATCH, MEM_LEN, D_MODEL), f32)
    offs = jax.random.randint(next(ks), (BATCH, 1), 0, 1024, dtype=jnp.int32)
    positions = offs + jnp.arange(SEQ, dtype=jnp.int32)[None, :]
    return {
        'x': x,
        'mem': mem,
        'positions': positions,
        'g_mix': gain((L, D_MODEL)),
        'w_in': nrm((L, D_MODEL, IN_PROJ_COLS), D_MODEL ** -0.5),
        'g_q': gain((L, Q_LORA_RANK)),
        'w_uq': nrm((L, Q_LORA_RANK, MLA_HEADS * (QK_NOPE_DIM + QK_ROPE_DIM)), Q_LORA_RANK ** -0.5),
        'g_kv': gain((L, KV_LORA_RANK)),
        'w_ukv': nrm((L, KV_LORA_RANK, MLA_HEADS * (QK_NOPE_DIM + V_HEAD_DIM)), KV_LORA_RANK ** -0.5),
        'conv_w': nrm((L, CONV_WIDTH, CONV_DIM), CONV_WIDTH ** -0.5),
        'g_out': gain((L, MIX_WIDTH)),
        'w_o': nrm((L, MIX_WIDTH, D_MODEL), MIX_WIDTH ** -0.5),
        'g_x': gain((L, D_MODEL)),
        'g_mem': gain((L, D_MODEL)),
        'w_xq': nrm((L, D_MODEL, D_MODEL), D_MODEL ** -0.5),
        'w_xkv': nrm((L, D_MODEL, 2 * D_MODEL), D_MODEL ** -0.5),
        'w_xo': nrm((L, D_MODEL, D_MODEL), D_MODEL ** -0.5),
        'g_ffn': gain((L, D_MODEL)),
        'w_pq': nrm((L, D_MODEL, PEER_HEADS * PEER_QDIM), D_MODEL ** -0.5),
        'sub_keys': nrm((L, PEER_HEADS, 2, PEER_KEYS, PEER_QDIM // 2), (PEER_QDIM // 2) ** -0.5),
        'u_experts': nrm((L, PEER_EXPERTS, D_MODEL), D_MODEL ** -0.5),
        'v_experts': nrm((L, PEER_EXPERTS, D_MODEL), PEER_HEADS ** -0.5),
        'g_final': gain((D_MODEL,)),
    }

def reference(x, mem, positions, g_mix, w_in, g_q, w_uq, g_kv, w_ukv, conv_w, g_out, w_o,
              g_x, g_mem, w_xq, w_xkv, w_xo, g_ffn, w_pq, sub_keys, u_experts, v_experts, g_final):
    cos, sin = rope_tables(positions, QK_ROPE_DIM, x.dtype)
    h = x
    for l in range(DEPTH):
        h = h + mixer_block(rmsnorm(h, g_mix[l]), cos, sin, w_in[l], g_q[l], w_uq[l],
                            g_kv[l], w_ukv[l], conv_w[l], g_out[l], w_o[l])
        h = h + memory_xattn(rmsnorm(h, g_x[l]), rmsnorm(mem, g_mem[l]),
                             w_xq[l], w_xkv[l], w_xo[l])
        h = h + peer_ffn(rmsnorm(h, g_ffn[l]), w_pq[l], sub_keys[l], u_experts[l], v_experts[l])
    return rmsnorm(h, g_final)


_drawn_inputs = setup_inputs


def setup_inputs(seed=0):
    import zlib

    import numpy as np

    out = dict(_drawn_inputs(seed))
    spreads = {}
    factors = {'g_q': 3.173, 'g_out': 2.716, 'g_x': 8.0, 'g_mem': 8.0, 'g_ffn': 22.886, 'g_final': 7.96}
    for name, (base, spread) in spreads.items():
        noise = np.random.default_rng([zlib.crc32(name.encode()), seed]).standard_normal(out[name].shape)
        drawn = base * np.exp(spread * noise) if base else spread * noise
        out[name] = __import__('jax').numpy.asarray(drawn.astype(out[name].dtype))
    for name, factor in factors.items():
        out[name] = (out[name] * factor).astype(out[name].dtype)
    return out
```

```python
import math
from contextlib import ExitStack

import concourse.bass as bass
from concourse import mybir

F32 = mybir.dt.float32
BF16 = mybir.dt.bfloat16
U32 = mybir.dt.uint32
I32 = mybir.dt.int32
ALU = mybir.AluOpType
ACT = mybir.ActivationFunctionType
AX_X = mybir.AxisListType.X

P = 128
SEQ = 1024
D = 1024
KT = D // P
BLOCKS = SEQ // P
MEM = 256
HEADS = 8
NOPE, ROPE, VDIM = 64, 32, 64
HALF = ROPE // 2
QK = NOPE + ROPE
QRANK, KVRANK = 384, 256
QT, KVT = QRANK // P, KVRANK // P
CONV = 512
TAPS = 3
GROUPS, GDIM = 16, 64
XHEADS, XDIM = 4, 256
PHEADS, PKEYS, PDIM = 8, 128, 64
TOPK = 16
EXPERTS = PHEADS * TOPK
EPS = 1e-6
NEG = -1e30
LOWEST = -3e38
ROUNDER = 1.5 * 2 ** 23
TURN_PARTS = (6.28125, 0.0019350051879882812, 2 * math.pi - 6.28125 - 0.0019350051879882812)
PI_BELOW = 3.1415925
HALFC = 512

RING = 8
STEPS_A_CUT = 4
CUTS = EXPERTS // STEPS_A_CUT
IDX_RING = 16
WRING = 3
WCHUNK = 2048
DIAGS = 4

RECTS = [(0, 1, 16), (1, 1, 8), (2, 2, 5), (4, 4, 3), (8, 8, 1)]
CAND = sum(ni * nj for _, ni, nj in RECTS)

MIX, LORA, MIXED, CROSS, PROBS, FFN, PEERQ = range(7)
TURNS = 7
MEM_TURNS = 2
R_MIX, R_LORA, R_GROUP, R_CROSS, R_FFN = range(5)
ROOTS = 5
MEM_ROOTS = 2
POOL_CONSTS = 15
PRE_CHUNKS = 16
G_MIX, G_Q, G_KV, G_OUT, G_X, G_MEM = 0, KT, KT + QT, KT + QT + KVT, 2 * KT + QT + KVT, 3 * KT + QT + KVT
G_COLS = 4 * KT + QT + KVT


def block_chunks(w):
    return ([(w["w_cq"], c, 4 * QRANK) for c in range(2)]
            + [(w["w_ckvr"], c, 4 * (KVRANK + ROPE)) for c in range(2)]
            + [(w["w_conv"], c, WCHUNK) for c in range(6)]
            + [(w["w_uq"], c, QT * QRANK) for c in range(2)]
            + [(w["w_ukv"], 0, KVT * D)]
            + [(w["w_o"], c, WCHUNK) for c in range(4)]
            + [(w["cross_a"], c, WCHUNK) for c in range(4)]
            + [(w["cross_b"], c, WCHUNK) for c in range(4)]
            + [(w["w_pq"], c, WCHUNK) for c in range(4)]
            + [(w["keys"], 0, PHEADS * PKEYS)])


C_CQ, C_CKVR, C_CONV, C_UQ, C_UKV, C_O, C_A, C_B, C_PQ, C_KEYS = 0, 2, 4, 10, 12, 13, 17, 21, 25, 29
CHUNKS = 30
assert CHUNKS % WRING == 0


def layer_kernel(nc, w, out):
    ctx = ExitStack()
    with ctx:
        def sb(name, shape, dt=F32):
            return ctx.enter_context(nc.sbuf_tensor(name, shape, dt))

        def pb(name, shape):
            return ctx.enter_context(nc.psum_tensor(name, shape, F32))

        def sem(name):
            return ctx.enter_context(nc.semaphore(name))

        rows = sb("rows", [P, RING, 2 * D])
        wbuf = sb("wbuf", [P, WRING, WCHUNK])
        kT = sb("kT", [QK, HEADS, SEQ])
        vals = sb("vals", [P, BLOCKS, HEADS * VDIM])
        big = sb("big", [P, 2, D])
        big2 = sb("big2", [P, 2, D])
        h = sb("h", [P, D])
        tile = sb("tile", [P, D])
        turned = sb("turned", [P, D])
        hn = sb("hn", [P, D])
        g_ffn = sb("g_ffn_b", [P, D])
        g_fin = sb("g_fin_b", [P, D])
        convw = sb("convw", [P, TAPS, CONV])
        tail = sb("tail", [P, 2, CONV])
        qk = sb("qk", [P, 2 * HEADS, QK])
        tri = sb("tri", [P, SEQ + (BLOCKS - 1) * P], BF16)
        diag = sb("diag", [P, DIAGS, P])
        ident = sb("ident", [P, P])
        shift = sb("shift", [P, 2, P])
        carry = sb("carry", [P, 2, P])
        gcol = sb("gcol", [P, G_COLS])
        cos_t = sb("cos_t", [P, BLOCKS, HALF])
        sin_t = sb("sin_t", [P, BLOCKS, HALF])
        best_v = sb("best_v", [P, 2 * PHEADS, TOPK])
        best_i = sb("best_i", [P, 2 * PHEADS, TOPK], U32)
        best_f = sb("best_f", [P, 2 * PHEADS, TOPK])
        gates_next = sb("gates_next", [P, EXPERTS])
        gates = sb("gates", [P, EXPERTS])
        idx_next = sb("idx_next", [P, EXPERTS], U32)
        idx_cur = sb("idx_cur", [P, EXPERTS], U32)
        idx_ring = sb("idx_ring", [P, IDX_RING], U32)
        iota_c = sb("iota_c", [P, CAND])
        ss = sb("ss", [P, 40])
        std = sb("std", [P, 40])
        rinv = sb("rinv", [P, 40])
        mx = sb("mx", [P, HEADS])
        nmx = sb("nmx", [P, HEADS])
        rsum = sb("rsum", [P, HEADS])
        eps = sb("eps", [P, 1])
        dot = sb("dot", [P, RING])
        act_v = sb("act_v", [P, RING])
        act_g = sb("act_g", [P, RING])

        acc = pb("acc", [P, D])
        pT = pb("pT", [P, D])
        pM = pb("pM", [P, D])
        pS = pb("pS", [P, D])

        gate_c = big2[:, 0, 0:CONV]
        z = big2[:, 0, CONV:2 * CONV]
        lora = big2[:, 1, 0:QRANK + KVRANK + ROPE]
        taps = big[:].rearrange("p a d -> p (a d)")[:, 0:TAPS * CONV].rearrange("p (k d) -> p k d", k=TAPS)
        gate_b = big[:, 1, CONV:]
        rtmp = big2[:, 0, 0:4 * HEADS * HALF].rearrange("p (k h f) -> p k h f", k=2, h=2 * HEADS)
        top_p = best_i[:, 0:PHEADS, :]
        top_f = best_v[:, PHEADS:, :]
        top_m = best_v[:, 0:PHEADS, :]
        pscore = big[:].rearrange("p a d -> p (a d)").rearrange("p (s n) -> p s n", s=2 * PHEADS)
        rest = big2[:, 0, :].rearrange("p (s n) -> p s n", s=8)
        qk_flat = qk[:].rearrange("p a d -> p (a d)")
        cand_v = qk_flat[:, 0:PHEADS * CAND].rearrange("p (h c) -> p h c", h=PHEADS)
        cand_i = qk_flat[:, PHEADS * CAND:2 * PHEADS * CAND].rearrange("p (h c) -> p h c", h=PHEADS)
        cand_r = qk_flat[:, 2 * PHEADS * CAND:3 * PHEADS * CAND].rearrange("p (h c) -> p h c", h=PHEADS)
        top_v = qk_flat[:, 3 * PHEADS * CAND:3 * PHEADS * CAND + EXPERTS].rearrange("p (h k) -> p h k", h=PHEADS)
        hit = [big2[:, s, 0:TOPK * CAND].rearrange("p (k c) -> p k c", k=TOPK) for s in range(2)]
        qT = turned[0:QK, :].rearrange("p (h t) -> p h t", h=HEADS)
        turned3 = turned[:].rearrange("p (k t) -> p k t", k=KT)
        pT3 = pT[:].rearrange("p (k t) -> p k t", k=KT)
        pS3 = pS[:].rearrange("p (k t) -> p k t", k=KT)
        out_stage = big2[:, 1, :]
        memT = rows[:, 0, :].rearrange("p (k m) -> p k m", k=KT)
        xkT = rows[:, 1, :].rearrange("p (k m) -> p k m", k=KT)
        xvT = rows[:, 2, :].rearrange("p (k m) -> p k m", k=KT)
        fold = [rows[:, 3 + s, :].rearrange("p (k m) -> p k m", k=4) for s in range(2)]
        memx = rows[:, 5:7, 0:D]
        ang = rows[:, 7, 0:4 * P].rearrange("p (k b f) -> p k b f", k=4, b=BLOCKS)
        posf = rows[:, 7, 4 * P:4 * P + BLOCKS]
        invf = rows[:, 7, 5 * P:5 * P + HALF]
        posi = rows[:, 7, 6 * P:6 * P + BLOCKS].bitcast(I32)

        consts_in = sem("consts_in")
        gains_in = sem("gains_in")
        mem_in = sem("mem_in")
        x_in = sem("x_in")
        w_in = [sem(f"w_in{i}") for i in range(WRING)]
        w_done = sem("w_done")
        pool_set = sem("pool_set")
        angle_set = sem("angle_set")
        sincos_set = sem("sincos_set")
        dve_set = sem("dve_set")
        root_set = sem("root_set")
        tile_set = sem("tile_set")
        turn_set = sem("turn_set")
        turned_set = sem("turned_set")
        xkv_out = sem("xkv_out")
        fold_set = sem("fold_set")
        fold_out = sem("fold_out")
        fold_stored = [sem(f"fold_stored{s}") for s in range(2)]
        in_out = sem("in_out")
        z_set = sem("z_set")
        taps_set = sem("taps_set")
        conv_set = sem("conv_set")
        conv_out = sem("conv_out")
        tail_set = sem("tail_set")
        q_out = sem("q_out")
        kv_out = sem("kv_out")
        v_out = sem("v_out")
        qk_set = sem("qk_set")
        qk_turn = sem("qk_turn")
        qT_set = sem("qT_set")
        kT_set = sem("kT_set")
        score_set = sem("score_set")
        masked_set = sem("masked_set")
        prob_set = sem("prob_set")
        prob_turn = sem("prob_turn")
        probT_set = sem("probT_set")
        head_out = sem("head_out")
        gsum_set = sem("gsum_set")
        h_mix = sem("h_mix")
        xmax_set = sem("xmax_set")
        xexp_set = sem("xexp_set")
        h_cross = sem("h_cross")
        pscore_out = sem("pscore_out")
        gate_in = sem("gate_in")
        gate_exp = sem("gate_exp")
        chosen = sem("chosen")
        idx_taken = sem("idx_taken")
        gates_taken = sem("gates_taken")
        hn_taken = sem("hn_taken")
        h_taken = sem("h_taken")
        pool_past = sem("pool_past")
        sp_past = sem("sp_past")
        dve_past = sem("dve_past")
        idx_staged = sem("idx_staged")
        rows_in = [sem(f"rows_in{i}") for i in range(RING)]
        ring_open = sem("ring_open")
        dot_set = sem("dot_set")
        diag_set = sem("diag_set")
        acc_out = sem("acc_out")
        final_root = sem("final_root")
        out_set = sem("out_set")
        out_stored = sem("out_stored")

        block = ctx.enter_context(nc.Block())

        def turn_no(b, stage):
            return b * TURNS + MEM_TURNS + stage + 1

        def root_no(b, stage):
            return b * ROOTS + MEM_ROOTS + stage + 1

        def chunk_slot(c):
            return (PRE_CHUNKS + c) % WRING

        def chunk_in(eng, b, c):
            eng.wait_ge(w_in[chunk_slot(c)],
                        b * (16 * CHUNKS // WRING) + 16 * ((PRE_CHUNKS + c) // WRING + 1))

        def multiplied(eng, b, c):
            eng.wait_ge(w_done, b * CHUNKS + PRE_CHUNKS + c + 1)

        def pre_chunk_in(eng, c):
            eng.wait_ge(w_in[c % WRING], 16 * (c // WRING + 1))

        @block.sync
        def _(sp):
            for name, dst in (("gcol", gcol[:]), ("pos", posi)):
                sp.dma_start(dst, w[name]).then_inc(consts_in, 16)
            sp.dma_start(invf, w["inv_freq"].to_broadcast([P, HALF])).then_inc(consts_in, 16)
            sp.dma_start(memx, w["mem"].rearrange("(m p) d -> p m d", p=P)).then_inc(mem_in, 16)

            def pre_chunk(n, src):
                if n >= WRING:
                    sp.wait_ge(w_done, n - WRING + 1)
                sp.dma_start(wbuf[:, n % WRING, :], src).then_inc(w_in[n % WRING], 16)

            n = 0
            for name, count in (("w_xkv", 8), ("w_xqT", 4), ("w_xo", 4)):
                for c in range(count):
                    pre_chunk(n, w[name][c])
                    n += 1
            sp.dma_start(g_ffn[:], w["g_ffn"].to_broadcast([P, D])).then_inc(gains_in, 16)
            sp.dma_start(g_fin[:], w["g_final"].to_broadcast([P, D])).then_inc(gains_in, 16)
            sp.dma_start(convw[:].rearrange("p k d -> p (k d)"), w["conv_w"].to_broadcast([P, TAPS * CONV])).then_inc(gains_in, 16)

            def loads(b, first):
                if not first:
                    sp.wait_ge(h_taken, b)
                sp.dma_start(h[:], w["x"][bass.ds(b * P, P), :]).then_inc(x_in, 16)
                for c, (src, k, cols) in enumerate(block_chunks(w)):
                    if first and c == C_A:
                        for s in range(2):
                            sp.wait_ge(fold_stored[s], 16 * 4)
                    sp.wait_ge(w_done, b * CHUNKS + PRE_CHUNKS + c - WRING + 1)
                    sp.dma_start(wbuf[:, chunk_slot(c), 0:cols], src[k]).then_inc(w_in[chunk_slot(c)], 16)

            def store(b):
                sp.wait_ge(out_set, b + 1)
                sp.dma_start(out[bass.ds(b * P, P), :], out_stage).then_inc(out_stored, 16)
                sp.wait_ge(out_stored, b * 16 + 16)
                sp.sem_inc(sp_past, 1)

            loads(0, True)
            with sp.Fori(1, BLOCKS) as b:
                loads(b, False)
                store(b - 1)
            store(BLOCKS - 1)
            for s in range(2):
                sp.wait_ge(fold_stored[s], 16 * 4)

        @block.gpsimd
        def _(pool):
            done = [0]

            def made(ins):
                done[0] += 1
                ins.then_inc(pool_set, 1)

            made(pool.memset(ident[:], 0.0))
            made(pool.memset(shift[:], 0.0))
            made(pool.memset(carry[:], 0.0))
            made(pool.memset(tri[:], 0.0))
            pool.wait_ge(pool_set, done[0])
            made(pool.affine_select(out=ident[:], in_=ident[:], compare_op=ALU.not_equal, fill=1.0, base=0,
                                    pattern=[[-1, P]], channel_multiplier=1))
            for k in range(2):
                made(pool.affine_select(out=shift[:, k, :], in_=shift[:, k, :], compare_op=ALU.not_equal, fill=1.0,
                                        base=1 + k, pattern=[[-1, P]], channel_multiplier=1))
                made(pool.affine_select(out=carry[:, k, :], in_=carry[:, k, :], compare_op=ALU.not_equal, fill=1.0,
                                        base=1 + k - P, pattern=[[-1, P]], channel_multiplier=1))
            made(pool.affine_select(out=tri[:], in_=tri[:], compare_op=ALU.is_ge, fill=NEG, base=(BLOCKS - 1) * P,
                                    pattern=[[-1, SEQ + (BLOCKS - 1) * P]], channel_multiplier=1))
            made(pool.iota(idx_next[:, 0:CAND], pattern=[[1, CAND]], base=0, channel_multiplier=0))
            pool.wait_ge(pool_set, done[0])
            made(pool.tensor_copy(iota_c[:], idx_next[:, 0:CAND]))
            made(pool.memset(tail[:], 0.0))
            made(pool.memset(kT[:], 0.0))
            made(pool.memset(vals[:], 0.0))
            assert done[0] == POOL_CONSTS

            with pool.Fori(0, BLOCKS) as b:
                pool.wait_ge(chosen, b + 1)
                pool.sem_inc(pool_past, 1)
                pool.tensor_copy(idx_cur[:], idx_next[:]).then_inc(idx_taken, 1)
                pool.wait_ge(idx_taken, b + 1)
                pool.sem_inc(pool_past, 1)
                with pool.Fori(0, EXPERTS // IDX_RING) as r:
                    for g in range(IDX_RING // 4):
                        cols = slice(4 * g, 4 * g + 4)
                        pool.tensor_copy(idx_ring[:, cols], idx_cur[:, bass.ds(r * IDX_RING + 4 * g, 4)])\
                            .then_inc(idx_staged, 1)
                        pool.wait_ge(idx_staged, b * (EXPERTS // 4) + r * (IDX_RING // 4) + g + 1)
                        for k in range(4 * g, 4 * g + 4):
                            pool.wait_ge(ring_open, b * EXPERTS + r * IDX_RING + k + 1)
                            pool.sem_inc(pool_past, 1)
                            pool.indirect_dma_start(
                                out=rows[:, k % RING, :], out_offset=None, in_=w["experts"][:, :],
                                in_offset=bass.IndirectOffsetOnAxis(ap=idx_ring[:, k:k + 1], axis=0),
                            ).then_inc(rows_in[k % RING], 16)
        @block.scalar
        def _(act):
            def steps(b, rnd, par):
                first = par * STEPS_A_CUT
                slots = range(first, first + STEPS_A_CUT)
                n = b * EXPERTS + rnd * RING + first
                act.wait_ge(dot_set, n + STEPS_A_CUT)
                act.activation(act_v[:, first:first + STEPS_A_CUT], dot[:, first:first + STEPS_A_CUT],
                               ACT.Gelu_apprx_tanh)
                act.drain()
                for s in slots:
                    act.activation(act_g[:, s:s + 1], gates[:, bass.ds(rnd * RING + s, 1)], ACT.Copy,
                                   scale=act_v[:, s:s + 1])
                act.drain()
                act.wait_ge(ring_open, n + STEPS_A_CUT + RING - DIAGS)
                for s in slots:
                    act.activation(diag[:, s % DIAGS, :], ident[:], ACT.Copy, scale=act_g[:, s:s + 1])\
                        .then_inc(diag_set, 1)

            def root(src, col, width, n=1, junk=None):
                act.activation(junk, src, ACT.Square, accum_out=ss[:, col:col + n])

            def roots(col, n, width):
                act.drain()
                return act.activation(std[:, col:col + n], ss[:, col:col + n], ACT.Sqrt, bias=eps[:, 0:1],
                                      scale=1.0 / width)

            def front(b, keys, cut):
                cut(0)
                act.wait_ge(x_in, b * 16 + 16)
                if keys > 1:
                    act.wait_ge(hn_taken, b)
                root(h[:], 0, D, junk=tile[:])
                roots(0, 1, D).then_inc(root_set, 1)
                cut(1)
                cut(2)
                multiplied(act, b, C_CQ + 1)
                act.copy(lora[:, 0:QRANK], pM[:, 0:QRANK]).then_inc(in_out, 1)
                multiplied(act, b, C_CQ + 3)
                act.copy(lora[:, QRANK:], pM[:, HALFC:HALFC + KVRANK + ROPE]).then_inc(in_out, 1)
                act.drain()
                root(lora[:, 0:QRANK], 1, QRANK, junk=tile[:, 0:QRANK])
                root(lora[:, QRANK:QRANK + KVRANK], 2, KVRANK, junk=tile[:, QRANK:QRANK + KVRANK])
                roots(1, 1, QRANK)
                act.activation(std[:, 2:3], ss[:, 2:3], ACT.Sqrt, bias=eps[:, 0:1], scale=1.0 / KVRANK)\
                    .then_inc(root_set, 1)
                cut(3)
                multiplied(act, b, C_CONV + 1)
                act.copy(gate_c, pM[:, 0:HALFC]).then_inc(in_out, 1)
                cut(4)
                multiplied(act, b, C_CONV + 5)
                act.copy(gate_b, pM[:, 0:HALFC]).then_inc(in_out, 1)
                cut(5)
                multiplied(act, b, C_UQ + 1)
                act.copy(qk[:, 0:4, :], pM[:, 0:QRANK].rearrange("p (h d) -> p h d", h=4))
                act.copy(qk[:, 4:8, :], pM[:, HALFC:HALFC + QRANK].rearrange("p (h d) -> p h d", h=4))\
                    .then_inc(q_out, 1)
                multiplied(act, b, C_UKV)
                act.wait_ge(v_out, b + 1)
                kv = pS[:].rearrange("p (h d) -> p h d", h=HEADS)
                act.copy(qk[:, HEADS:, 0:NOPE], kv[:, :, 0:NOPE]).then_inc(kv_out, 1)
                cut(6)
                act.wait_ge(conv_set, b + 1)
                act.copy(tail[:], taps[:, 0:2, :]).then_inc(tail_set, 1)
                act.wait_ge(qk_turn, b * 2 + 1)
                act.copy(qT, pT3[0:QK, :, :]).then_inc(qT_set, 1)

                def exps(hd):
                    act.wait_ge(masked_set, b * HEADS + hd + 1)
                    act.activation(big[:, hd % 2, 0:keys * P], big[:, hd % 2, 0:keys * P], ACT.Exp,
                                   bias=nmx[:, hd:hd + 1], scale=1.0 / math.sqrt(QK),
                                   accum_out=rsum[:, hd:hd + 1]).then_inc(prob_set, 1)

                def probT(hd):
                    act.wait_ge(prob_turn, b * HEADS + hd + 1)
                    if hd >= 2:
                        act.wait_ge(head_out, b * HEADS + hd - 1)
                    act.copy(big2[:, hd % 2, 0:keys * P], pT[:, 0:keys * P]).then_inc(probT_set, 1)

                for c in range(HEADS // 2 + 1):
                    cut(7 + c)
                    for it in (2 * c, 2 * c + 1):
                        if 1 <= it <= HEADS:
                            probT(it - 1)
                        if it < HEADS:
                            exps(it)
                cut(12)
                act.wait_ge(gsum_set, b + 1)
                act.activation(std[:, 8:8 + GROUPS], ss[:, 8:8 + GROUPS], ACT.Sqrt, bias=eps[:, 0:1],
                               scale=1.0 / GDIM).then_inc(root_set, 1)
                cut(13)
                cut(14)
                act.wait_ge(h_mix, b * 2 + 2)
                root(h[:], 3, D, junk=tile[:])
                roots(3, 1, D).then_inc(root_set, 1)
                cut(15)
                cut(16)
                act.wait_ge(xmax_set, b + 1)
                for hd in range(XHEADS):
                    ins = act.activation(tile[:, hd * MEM:(hd + 1) * MEM], pM[:, hd * MEM:(hd + 1) * MEM], ACT.Exp,
                                         bias=nmx[:, hd:hd + 1], scale=1.0 / math.sqrt(XDIM),
                                         accum_out=rsum[:, hd:hd + 1])
                ins.then_inc(xexp_set, 1)
                cut(17)
                cut(18)
                act.wait_ge(h_cross, b * 2 + 2)
                root(h[:], 4, D, junk=big[:, 0, :])
                roots(4, 1, D).then_inc(root_set, 1)
                cut(19)
                cut(20)
                multiplied(act, b, C_PQ + 3)
                act.copy(big[:, 1, :], pM[:]).then_inc(tile_set, 1)
                cut(21)
                cut(22)
                multiplied(act, b, C_KEYS)
                flat = big[:].rearrange("p a d -> p (a d)")
                act.copy(flat[:, 0:D], pS[:])
                act.copy(flat[:, D:2 * D], pM[:]).then_inc(pscore_out, 1)
                for c in range(23, 29):
                    cut(c)
                act.wait_ge(gate_in, b + 1)
                act.activation(top_f, top_m, ACT.Exp).then_inc(gate_exp, 1)
                for c in range(29, CUTS):
                    cut(c)

            def boundary(b):
                act.wait_ge(chosen, b + 1)
                act.copy(gates[:], gates_next[:]).then_inc(gates_taken, 1)
                act.drain()

            def finish(b):
                act.wait_ge(acc_out, b + 1)
                root(out_stage, 5, D, junk=big2[:, 0, :])
                roots(5, 1, D).then_inc(final_root, 1)

            act.wait_ge(dve_set, 1)
            act.wait_ge(pool_set, POOL_CONSTS)
            act.wait_ge(angle_set, 1)
            act.activation(sin_t[:], ang[:, 2], ACT.Sin)
            act.activation(cos_t[:], ang[:, 3], ACT.Sin).then_inc(sincos_set, 1)
            act.wait_ge(mem_in, 16)
            for m in range(2):
                if m == 1:
                    act.wait_ge(turn_set, 1)
                root(memx[:, m, :], 6 + m, D, junk=tile[:])
                roots(6 + m, 1, D).then_inc(root_set, 1)
            for n in range(4):
                act.wait_ge(w_done, 2 * n + 2)
                dst = (xkT, xvT)[n // 2][:, 4 * (n % 2):4 * (n % 2) + 4, :]
                act.copy(dst, (pM, pS)[n % 2][:].rearrange("p (k m) -> p k m", k=4)).then_inc(xkv_out, 1)
            n = 0
            for name in ("cross_a", "cross_b"):
                for half in range(2):
                    for q in range(2):
                        c = 2 * half + q if name == "cross_a" else 2 * q + half
                        s = n // 4 % 2
                        if n >= 8:
                            act.wait_ge(fold_stored[s], 16 * (n // 8))
                        for k in range(4):
                            if q == 1 and k == 3:
                                act.wait_ge(w_done, 8 + 2 * (n // 8) + 2)
                            else:
                                act.wait_ge(fold_set, n + 1 - n // 8)
                            act.copy(fold[s][:, k, :], (pM, pS)[n % 4 // 2][:, n % 2 * HALFC:n % 2 * HALFC + HALFC])\
                                .then_inc(fold_out, 1)
                            n += 1
                        act.wait_ge(fold_out, n)
                        act.dma_start(w[name][c], rows[:, 3 + s, :]).then_inc(fold_stored[s], 16)

            front(0, 1, lambda c: None)
            boundary(0)
            with act.Fori(1, BLOCKS) as b:
                front(b, BLOCKS, lambda c: steps(b - 1, c // 2, c % 2))
                boundary(b)
                finish(b - 1)
            with act.Fori(0, CUTS // 2) as r:
                for par in range(2):
                    steps(BLOCKS - 1, r, par)
            finish(BLOCKS - 1)


        @block.tensor
        def _(pe):
            def steps(b, rnd, par):
                for i in range(STEPS_A_CUT):
                    s = par * STEPS_A_CUT + i
                    pe.wait_ge(diag_set, b * EXPERTS + rnd * RING + s + 1)
                    for half in range(2):
                        cols = slice(half * HALFC, (half + 1) * HALFC)
                        mm = pe.matmul(acc[:, cols], diag[:, s % DIAGS, :],
                                       rows[:, s, D + half * HALFC:D + (half + 1) * HALFC],
                                       start=False, stop=False, skip_group_check=True)
                    mm.then_inc(ring_open, 1)

            def turn(src, b, stage, tiles=KT):
                pe.wait_ge(tile_set, turn_no(b, stage))
                for k in range(tiles):
                    tr = pe.transpose(pT3[:, k, :], src[:, k * P:(k + 1) * P], ident[:])
                tr.then_inc(turn_set, 1)

            def project(b, c, half, first_tile=0, width=HALFC, bank=None):
                bank = half if bank is None else bank
                for q in range(2):
                    chunk_in(pe, b, c + q)
                    for k in range(4):
                        mm = pe.matmul(pM[:, bank * HALFC:bank * HALFC + width], turned3[:, 4 * q + k, :],
                                       wbuf[:, chunk_slot(c + q), k * width:(k + 1) * width],
                                       start=(q == 0 and k == 0), stop=(q == 1 and k == 3))
                    mm.then_inc(w_done, 1)
                return mm

            def front(b, keys, cut):
                cut(0)
                turn(tile[:], b, MIX)
                cut(1)
                pe.wait_ge(turned_set, turn_no(b, MIX))
                project(b, C_CQ, 0, width=QRANK, bank=0)
                project(b, C_CQ + 2, 0, width=KVRANK + ROPE, bank=1)
                cut(2)
                pe.wait_ge(in_out, b * 4 + 1)
                project(b, C_CONV, 0, bank=0)
                pe.wait_ge(in_out, b * 4 + 2)
                project(b, C_CONV + 2, 0, bank=1)
                cut(3)
                pe.wait_ge(in_out, b * 4 + 3)
                project(b, C_CONV + 4, 0, bank=0)
                turn(tile[:], b, LORA, QT + KVT)
                cut(4)
                pe.wait_ge(turned_set, turn_no(b, LORA))
                pe.wait_ge(in_out, b * 4 + 4)
                pe.wait_ge(z_set, b + 1)
                for half in range(2):
                    chunk_in(pe, b, C_UQ + half)
                    for k in range(QT):
                        mm = pe.matmul(pM[:, half * HALFC:half * HALFC + QRANK], turned3[:, k, :],
                                       wbuf[:, chunk_slot(C_UQ + half), k * QRANK:(k + 1) * QRANK],
                                       start=(k == 0), stop=(k == QT - 1))
                    mm.then_inc(w_done, 1)
                chunk_in(pe, b, C_UKV)
                for half in range(2):
                    for k in range(KVT):
                        mm = pe.matmul(pS[:, half * HALFC:(half + 1) * HALFC], turned3[:, QT + k, :],
                                       wbuf[:, chunk_slot(C_UKV), k * D + half * HALFC:k * D + (half + 1) * HALFC],
                                       start=(k == 0), stop=(k == KVT - 1))
                mm.then_inc(w_done, 1)
                cut(5)
                pe.wait_ge(q_out, b + 1)
                pe.wait_ge(taps_set, b + 1)
                if keys > 1:
                    pe.wait_ge(tail_set, b)
                pe.matmul(pM[:, 0:CONV], ident[:], taps[:, 2, :], start=True, stop=False)
                for k in range(2):
                    pe.matmul(pM[:, 0:CONV], shift[:, k, :], taps[:, 1 - k, :], start=False, stop=False)
                    mm = pe.matmul(pM[:, 0:CONV], carry[:, k, :], tail[:, 1 - k, :], start=False, stop=(k == 1))
                mm.then_inc(conv_set, 1)
                pe.wait_ge(qk_set, b + 1)
                for hd in range(HEADS):
                    tr = pe.transpose(pT3[0:QK, hd, :], qk[:, hd, :], ident[:])
                tr.then_inc(qk_turn, 1)
                pe.wait_ge(kv_out, b + 1)
                for hd in range(HEADS):
                    tr = pe.transpose(pS3[0:QK, hd, :], qk[:, HEADS + hd, :], ident[:])
                tr.then_inc(qk_turn, 1)
                cut(6)
                pe.wait_ge(qT_set, b + 1)
                pe.wait_ge(kT_set, b + 1)
                pe.wait_ge(conv_out, b + 1)
                pe.wait_ge(v_out, b + 1)

                def scores(hd):
                    if hd:
                        pe.wait_ge(masked_set, b * HEADS + hd)
                    for c in range(0, keys * P, HALFC):
                        n = min(HALFC, keys * P)
                        mm = pe.matmul(pS[:, c:c + n], qT[:, hd, :], kT[:, hd, c:c + n], start=True, stop=True)
                    mm.then_inc(score_set, 1)

                def turn_probs(hd):
                    pe.wait_ge(prob_set, b * HEADS + hd + 1)
                    if hd:
                        pe.wait_ge(probT_set, b * HEADS + hd)
                    for k in range(keys):
                        tr = pe.transpose(pT3[:, k, :], big[:, hd % 2, k * P:(k + 1) * P], ident[:])
                    tr.then_inc(prob_turn, 1)

                def weigh(hd):
                    pe.wait_ge(probT_set, b * HEADS + hd + 1)
                    for k in range(keys):
                        mm = pe.matmul(pM[:, hd * VDIM:(hd + 1) * VDIM], big2[:, hd % 2, k * P:(k + 1) * P],
                                       vals[:, k, hd * VDIM:(hd + 1) * VDIM], start=(k == 0), stop=(k == keys - 1))
                    mm.then_inc(head_out, 1)

                for c in range(HEADS // 2 + 1):
                    for it in (2 * c, 2 * c + 1):
                        if it < HEADS:
                            scores(it)
                        if 1 <= it <= HEADS:
                            turn_probs(it - 1)
                        if it >= 2:
                            weigh(it - 2)
                    cut(7 + c)
                cut(12)
                turn(tile[:], b, MIXED)
                cut(13)
                pe.wait_ge(turned_set, turn_no(b, MIXED))
                for half in range(2):
                    project(b, C_O + 2 * half, half)
                cut(14)
                turn(tile[:], b, CROSS)
                cut(15)
                pe.wait_ge(turned_set, turn_no(b, CROSS))
                for half in range(2):
                    project(b, C_A + 2 * half, half)
                cut(16)
                turn(tile[:], b, PROBS)
                cut(17)
                pe.wait_ge(turned_set, turn_no(b, PROBS))
                for half in range(2):
                    project(b, C_B + 2 * half, half)
                cut(18)
                turn(tile[:], b, FFN)
                cut(19)
                pe.wait_ge(turned_set, turn_no(b, FFN))
                for half in range(2):
                    project(b, C_PQ + 2 * half, half)
                cut(20)
                turn(big[:, 1, :], b, PEERQ)
                cut(21)
                pe.wait_ge(turned_set, turn_no(b, PEERQ))
                chunk_in(pe, b, C_KEYS)
                for hc in range(2 * PHEADS):
                    hd, c = hc // 2, hc % 2
                    mm = pe.matmul((pS, pM)[c][:, hd * PKEYS:(hd + 1) * PKEYS], turned3[c * PDIM:(c + 1) * PDIM, hd, :],
                                   wbuf[c * PDIM:(c + 1) * PDIM, chunk_slot(C_KEYS), hd * PKEYS:(hd + 1) * PKEYS],
                                   start=True, stop=True)
                mm.then_inc(w_done, 1)
                for c in range(22, CUTS):
                    cut(c)

            def boundary(b, first):
                if not first:
                    pe.wait_ge(acc_out, b)
                pe.wait_ge(h_cross, 2 * b + 2)
                for half in range(2):
                    cols = slice(half * HALFC, (half + 1) * HALFC)
                    mm = pe.matmul(acc[:, cols], ident[:], h[:, cols], start=True, stop=False, skip_group_check=True)
                mm.then_inc(h_taken, 1)

            pe.sem_inc(ring_open, RING)
            pe.wait_ge(pool_set, POOL_CONSTS)
            for m in range(2):
                pe.wait_ge(tile_set, m + 1)
                if m:
                    pe.wait_ge(turned_set, m)
                for k in range(KT):
                    tr = pe.transpose(pT3[:, k, :], tile[:, k * P:(k + 1) * P], ident[:])
                tr.then_inc(turn_set, 1)
            pe.wait_ge(turned_set, 2)
            for n in range(4):
                if n >= 2:
                    pe.wait_ge(xkv_out, n - 1)
                for q in range(2):
                    pre_chunk_in(pe, 2 * n + q)
                dst = (pM, pS)[n % 2][:].rearrange("p (k m) -> p k m", k=4)
                for ct in range(4):
                    for k in range(KT):
                        chunk = wbuf[:, (2 * n + k // 4) % WRING, :]
                        mm = pe.matmul(dst[:, ct, :], chunk[:, k % 4 * HALFC + ct * P:k % 4 * HALFC + (ct + 1) * P],
                                       memT[:, k, :], start=(k == 0), stop=(k == KT - 1))
                mm.then_inc(w_done, 2)
            pe.wait_ge(xkv_out, 4)
            n = 0
            for mat in range(2):
                for pair in range(2):
                    first = 8 + 4 * mat + 2 * pair
                    for q in range(2):
                        pre_chunk_in(pe, first + q)
                    for q in range(2):
                        for k in range(4):
                            if n >= 4:
                                pe.wait_ge(fold_out, n - 3)
                            bank = (pM, pS)[n % 4 // 2][:, n % 2 * HALFC:(n % 2 + 1) * HALFC]
                            if mat == 0:
                                for hh in range(2):
                                    chunk = wbuf[:, (first + hh) % WRING, :]
                                    for dt in range(2):
                                        at = dt * D + (q * 4 + k) * P
                                        mm = pe.matmul(bank[:, hh * MEM:(hh + 1) * MEM], chunk[:, at:at + P],
                                                       xkT[:, (2 * pair + hh) * 2 + dt, :],
                                                       start=(dt == 0), stop=(dt == 1))
                            else:
                                chunk = wbuf[:, (first + k // 2) % WRING, :]
                                for dt in range(2):
                                    at = dt * D + q * HALFC
                                    mm = pe.matmul(bank, xvT[:, (2 * pair + k // 2) * 2 + dt, k % 2 * P:(k % 2 + 1) * P],
                                                   chunk[:, at:at + HALFC], start=(dt == 0), stop=(dt == 1))
                            if q == 1 and k == 3:
                                mm.then_inc(w_done, 2)
                            else:
                                mm.then_inc(fold_set, 1)
                            n += 1

            front(0, 1, lambda c: None)
            boundary(0, True)
            with pe.Fori(1, BLOCKS) as b:
                front(b, BLOCKS, lambda c: steps(b - 1, c // 2, c % 2))
                boundary(b, False)
            with pe.Fori(0, CUTS // 2) as r:
                for par in range(2):
                    steps(BLOCKS - 1, r, par)

        @block.vector
        def _(dve):
            def steps(b, rnd, par):
                for i in range(STEPS_A_CUT):
                    s = par * STEPS_A_CUT + i
                    dve.wait_ge(rows_in[s], b * (16 * EXPERTS // RING) + rnd * 16 + 16)
                    dve.tensor_tensor_reduce(out=rows[:, s, 0:D], in0=rows[:, s, 0:D], in1=hn[:], scale=1.0,
                                             scalar=0.0, op0=ALU.mult, op1=ALU.add,
                                             accum_out=dot[:, s:s + 1]).then_inc(dot_set, 1)

            def take_root(no, col, n=1):
                dve.wait_ge(root_set, no)
                dve.reciprocal(rinv[:, col:col + n], std[:, col:col + n])
                dve.drain()

            def out_of_turn(no, gain, tiles=KT, dst=None):
                dve.wait_ge(turn_set, no)
                dst = turned3[:, 0:tiles, :] if dst is None else dst
                if gain is None:
                    dve.tensor_copy(dst, pT3[:, 0:tiles, :]).then_inc(turned_set, 1)
                else:
                    g = gcol[:, gain:gain + tiles].unsqueeze(2).to_broadcast([P, tiles, P])
                    dve.tensor_tensor(dst, pT3[:, 0:tiles, :], g, ALU.mult).then_inc(turned_set, 1)

            def front(b, keys, cut):
                cut(0)
                take_root(root_no(b, R_MIX), 0)
                dve.tensor_scalar(tile[:], h[:], rinv[:, 0:1], None, ALU.mult).then_inc(tile_set, 1)
                cut(1)
                out_of_turn(turn_no(b, MIX), G_MIX)
                cut(2)
                take_root(root_no(b, R_LORA), 1, 2)
                dve.tensor_scalar(tile[:, 0:QRANK], lora[:, 0:QRANK], rinv[:, 1:2], None, ALU.mult)
                dve.tensor_scalar(tile[:, QRANK:QRANK + KVRANK], lora[:, QRANK:QRANK + KVRANK], rinv[:, 2:3], None,
                                  ALU.mult).then_inc(tile_set, 1)
                kr = lora[:, QRANK + KVRANK:].unsqueeze(1).to_broadcast([P, HEADS, ROPE])
                dve.tensor_copy(qk[:, HEADS:, NOPE:], kr)
                cut(3)
                multiplied(dve, b, C_CONV + 3)
                dve.wait_ge(in_out, b * 4 + 3)
                dve.tensor_tensor(z, gate_c, pM[:, HALFC:], ALU.mult).then_inc(z_set, 1)
                dve.drain()
                dve.tensor_tensor(taps, convw[:], z.unsqueeze(1).to_broadcast([P, TAPS, CONV]), ALU.mult)\
                    .then_inc(taps_set, 1)
                cut(4)
                out_of_turn(turn_no(b, LORA), G_Q, QT + KVT)
                cut(5)
                multiplied(dve, b, C_UKV)
                kv = pS[:].rearrange("p (h d) -> p h d", h=HEADS)
                dst = vals[:, bass.ds(b, 1), :].rearrange("p b (h d) -> p (b h) d", h=HEADS)
                dve.tensor_copy(dst, kv[:, :, NOPE:]).then_inc(v_out, 1)
                dve.wait_ge(q_out, b + 1)
                dve.wait_ge(kv_out, b + 1)
                t1, t2 = qk[:, :, NOPE:NOPE + HALF], qk[:, :, NOPE + HALF:]
                cos = cos_t[:, bass.ds(b, 1), :].to_broadcast([P, 2 * HEADS, HALF])
                sin = sin_t[:, bass.ds(b, 1), :].to_broadcast([P, 2 * HEADS, HALF])
                dve.tensor_tensor(rtmp[:, 0], t1, sin, ALU.mult)
                dve.tensor_tensor(rtmp[:, 1], t2, sin, ALU.mult)
                dve.drain()
                dve.tensor_tensor(t1, t1, cos, ALU.mult)
                dve.tensor_tensor(t2, t2, cos, ALU.mult)
                dve.drain()
                dve.tensor_tensor(t1, t1, rtmp[:, 1], ALU.subtract)
                dve.tensor_tensor(t2, t2, rtmp[:, 0], ALU.add).then_inc(qk_set, 1)
                cut(6)
                dve.wait_ge(conv_set, b + 1)
                dve.wait_ge(in_out, b * 4 + 4)
                dve.tensor_tensor(tile[:, CONV:], gate_b, pM[:, 0:CONV], ALU.mult).then_inc(conv_out, 1)
                dve.wait_ge(qk_turn, b * 2 + 2)
                dve.tensor_copy(kT[:, :, bass.ds(b * P, P)], pS3[0:QK, :, :]).then_inc(kT_set, 1)
                dve.wait_ge(tail_set, b + 1)

                def mask(hd):
                    dve.wait_ge(score_set, b * HEADS + hd + 1)
                    if hd == 0:
                        dve.sem_inc(dve_past, 1)
                    if hd >= 2:
                        dve.wait_ge(prob_turn, b * HEADS + hd - 1)
                    n = keys * P
                    dve.tensor_tensor(big[:, hd % 2, 0:n], pS[:, 0:n], tri[:, bass.ds((BLOCKS - 1 - b) * P, n)], ALU.add)
                    dve.drain()
                    dve.tensor_reduce(mx[:, hd:hd + 1], big[:, hd % 2, 0:n], AX_X, ALU.max)
                    dve.drain()
                    dve.tensor_scalar(nmx[:, hd:hd + 1], mx[:, hd:hd + 1], -1.0 / math.sqrt(QK), None, ALU.mult)\
                        .then_inc(masked_set, 1)

                for c in range(HEADS // 2):
                    cut(7 + c)
                    mask(2 * c)
                    mask(2 * c + 1)
                cut(11)
                cut(12)
                dve.wait_ge(head_out, b * HEADS + HEADS)
                dve.reciprocal(rinv[:, 32:32 + HEADS], rsum[:])
                dve.drain()
                dve.tensor_tensor(tile[:, 0:HEADS * VDIM].rearrange("p (h d) -> p h d", h=HEADS),
                                  pM[:, 0:HEADS * VDIM].rearrange("p (h d) -> p h d", h=HEADS),
                                  rinv[:, 32:32 + HEADS].unsqueeze(2).to_broadcast([P, HEADS, VDIM]), ALU.mult)
                dve.drain()
                dve.tensor_tensor(big[:, 0, :], tile[:], tile[:], ALU.mult)
                dve.drain()
                dve.tensor_reduce(ss[:, 8:8 + GROUPS], big[:, 0, :].rearrange("p (g d) -> p g d", g=GROUPS), AX_X,
                                  ALU.add).then_inc(gsum_set, 1)
                take_root(root_no(b, R_GROUP), 8, GROUPS)
                tile3 = tile[:].rearrange("p (g d) -> p g d", g=GROUPS)
                dve.tensor_tensor(tile3, tile3, rinv[:, 8:8 + GROUPS].unsqueeze(2).to_broadcast([P, GROUPS, GDIM]),
                                  ALU.mult).then_inc(tile_set, 1)
                cut(13)
                out_of_turn(turn_no(b, MIXED), G_OUT)
                cut(14)
                for half in range(2):
                    cols = slice(half * HALFC, (half + 1) * HALFC)
                    multiplied(dve, b, C_O + 2 * half + 1)
                    dve.tensor_tensor(h[:, cols], h[:, cols], pM[:, cols], ALU.add).then_inc(h_mix, 1)
                take_root(root_no(b, R_CROSS), 3)
                dve.tensor_scalar(tile[:], h[:], rinv[:, 3:4], None, ALU.mult).then_inc(tile_set, 1)
                cut(15)
                out_of_turn(turn_no(b, CROSS), G_X)
                cut(16)
                multiplied(dve, b, C_A + 3)
                dve.tensor_reduce(mx[:, 0:XHEADS], pM[:].rearrange("p (h m) -> p h m", h=XHEADS), AX_X, ALU.max)
                dve.drain()
                dve.tensor_scalar(nmx[:, 0:XHEADS], mx[:, 0:XHEADS], -1.0 / math.sqrt(XDIM), None, ALU.mult)\
                    .then_inc(xmax_set, 1)
                dve.wait_ge(xexp_set, b + 1)
                dve.reciprocal(rinv[:, 32:32 + XHEADS], rsum[:, 0:XHEADS])
                dve.drain()
                tile4 = tile[:].rearrange("p (h m) -> p h m", h=XHEADS)
                dve.tensor_tensor(tile4, tile4, rinv[:, 32:32 + XHEADS].unsqueeze(2).to_broadcast([P, XHEADS, MEM]),
                                  ALU.mult).then_inc(tile_set, 1)
                cut(17)
                out_of_turn(turn_no(b, PROBS), None)
                cut(18)
                for half in range(2):
                    cols = slice(half * HALFC, (half + 1) * HALFC)
                    multiplied(dve, b, C_B + 2 * half + 1)
                    dve.tensor_tensor(h[:, cols], h[:, cols], pM[:, cols], ALU.add).then_inc(h_cross, 1)
                take_root(root_no(b, R_FFN), 4)
                dve.scalar_tensor_tensor(out=tile[:], in0=h[:], scalar=rinv[:, 4:5], in1=g_ffn[:], op0=ALU.mult,
                                         op1=ALU.mult).then_inc(tile_set, 1)
                cut(19)
                out_of_turn(turn_no(b, FFN), None)
                cut(20)
                cut(21)
                out_of_turn(turn_no(b, PEERQ), None)
                cut(22)
                dve.wait_ge(pscore_out, b + 1)
                dve.sem_inc(dve_past, 1)
                for part in range(2):
                    cut(23 + part)
                    sets = range(8 * part, 8 * part + 8)
                    for s in sets:
                        dve.max(best_v[:, s, 0:8], pscore[:, s, :])
                    dve.drain()
                    for s in sets:
                        dve.max_index(best_i[:, s, 0:8], best_v[:, s, 0:8], pscore[:, s, :])
                        dve.match_replace(rest[:, s % 8, :], best_v[:, s, 0:8], pscore[:, s, :], LOWEST)
                    dve.drain()
                    for s in sets:
                        dve.max(best_v[:, s, 8:16], rest[:, s % 8, :])
                    dve.drain()
                    for s in sets:
                        dve.max_index(best_i[:, s, 8:16], best_v[:, s, 8:16], rest[:, s % 8, :])
                cut(25)
                dve.drain()
                dve.tensor_copy(best_f[:], best_i[:])
                dve.drain()
                f4 = best_f[:].rearrange("p (c h) k -> p h c k", h=PHEADS)
                v4 = best_v[:].rearrange("p (c h) k -> p h c k", h=PHEADS)
                dve.tensor_scalar(f4[:, :, 0, :], f4[:, :, 0, :], float(PKEYS), None, ALU.mult)
                dve.drain()
                at = 0
                for i0, ni, nj in RECTS:
                    for src, dst in ((v4, cand_v), (f4, cand_i)):
                        a = src[:, :, 0, i0:i0 + ni].unsqueeze(3).to_broadcast([P, PHEADS, ni, nj])
                        c = src[:, :, 1, 0:nj].unsqueeze(2).to_broadcast([P, PHEADS, ni, nj])
                        d = dst[:, :, at:at + ni * nj].rearrange("p h (i j) -> p h i j", i=ni)
                        dve.tensor_tensor(d, a, c, ALU.add)
                    at += ni * nj
                dve.drain()
                for hd in range(PHEADS):
                    dve.max(top_v[:, hd, 0:8], cand_v[:, hd, :])
                dve.drain()
                for hd in range(PHEADS):
                    dve.max_index(top_p[:, hd, 0:8], top_v[:, hd, 0:8], cand_v[:, hd, :])
                    dve.match_replace(cand_r[:, hd, :], top_v[:, hd, 0:8], cand_v[:, hd, :], LOWEST)
                dve.drain()
                for hd in range(PHEADS):
                    dve.max(top_v[:, hd, 8:16], cand_r[:, hd, :])
                dve.drain()
                for hd in range(PHEADS):
                    dve.max_index(top_p[:, hd, 8:16], top_v[:, hd, 8:16], cand_r[:, hd, :])
                dve.drain()
                dve.tensor_copy(top_f, top_p)
                dve.drain()
                chosen_f = best_f[:].rearrange("p s k -> p (s k)")[:, 0:EXPERTS]
                for c, heads in enumerate(((0, 1, 2), (3, 4, 5), (6, 7))):
                    cut(26 + c)
                    for hd in heads:
                        t = hit[hd % 2]
                        dve.tensor_tensor(t, iota_c[:].unsqueeze(1).to_broadcast([P, TOPK, CAND]),
                                          top_f[:, hd, :].unsqueeze(2).to_broadcast([P, TOPK, CAND]), ALU.is_equal)
                        dve.drain()
                        dve.tensor_tensor(t, t, cand_i[:, hd, :].unsqueeze(1).to_broadcast([P, TOPK, CAND]), ALU.mult)
                        dve.drain()
                        dve.tensor_reduce(chosen_f[:, hd * TOPK:(hd + 1) * TOPK], t, AX_X, ALU.add)
                dve.drain()
                if keys > 1:
                    dve.wait_ge(idx_taken, b)
                    dve.wait_ge(gates_taken, b)
                dve.tensor_copy(idx_next[:], chosen_f)
                dve.tensor_tensor(top_m, top_v, top_v[:, :, 0:1].to_broadcast([P, PHEADS, TOPK]), ALU.subtract)\
                    .then_inc(gate_in, 1)
                dve.wait_ge(gate_exp, b + 1)
                dve.tensor_reduce(mx[:], top_f, AX_X, ALU.add)
                dve.drain()
                dve.reciprocal(rinv[:, 32:32 + PHEADS], mx[:])
                dve.drain()
                dve.tensor_tensor(gates_next[:].rearrange("p (h k) -> p h k", h=PHEADS), top_f,
                                  rinv[:, 32:32 + PHEADS].unsqueeze(2).to_broadcast([P, PHEADS, TOPK]), ALU.mult)\
                    .then_inc(chosen, 1)
                for c in range(29, CUTS):
                    cut(c)

            def stage(b):
                dve.wait_ge(ring_open, b * EXPERTS + EXPERTS + RING)
                dve.tensor_copy(out_stage, acc[:]).then_inc(acc_out, 1)

            def finish(b):
                dve.wait_ge(final_root, b + 1)
                dve.reciprocal(rinv[:, 5:6], std[:, 5:6])
                dve.drain()
                dve.scalar_tensor_tensor(out=out_stage, in0=out_stage, scalar=rinv[:, 5:6], in1=g_fin[:], op0=ALU.mult,
                                         op1=ALU.mult).then_inc(out_set, 1)

            def boundary():
                dve.drain()
                dve.tensor_copy(hn[:], tile[:]).then_inc(hn_taken, 1)
                dve.drain()

            dve.memset(eps[:], EPS).then_inc(dve_set, 1)
            dve.wait_ge(pool_set, POOL_CONSTS)
            dve.wait_ge(consts_in, 48)
            dve.tensor_copy(posf, posi)
            dve.drain()
            a = [ang[:, k] for k in range(4)]
            dve.tensor_tensor(a[0], posf.unsqueeze(2).to_broadcast([P, BLOCKS, HALF]),
                              invf.unsqueeze(1).to_broadcast([P, BLOCKS, HALF]), ALU.mult)
            dve.drain()
            dve.tensor_scalar(a[1], a[0], 1.0 / (2 * math.pi), ROUNDER, ALU.mult, ALU.add)
            dve.drain()
            dve.tensor_scalar(a[1], a[1], ROUNDER, None, ALU.subtract)
            dve.drain()
            for part in TURN_PARTS:
                dve.scalar_tensor_tensor(out=a[0], in0=a[1], scalar=-part, in1=a[0], op0=ALU.mult, op1=ALU.add)
                dve.drain()
            dve.tensor_scalar(a[2], a[0], PI_BELOW, -PI_BELOW, ALU.min, ALU.max)
            dve.drain()
            dve.scalar_tensor_tensor(out=a[3], in0=a[2], scalar=-1.0, in1=a[2], op0=ALU.mult, op1=ALU.max)
            dve.drain()
            dve.tensor_scalar(a[3], a[3], -1.0, math.pi / 2, ALU.mult, ALU.add).then_inc(angle_set, 1)
            for m in range(2):
                take_root(m + 1, 6 + m)
                dve.tensor_scalar(tile[:], memx[:, m, :], rinv[:, 6 + m:7 + m], None, ALU.mult).then_inc(tile_set, 1)
                out_of_turn(m + 1, G_MEM, dst=memT[:, :, m * P:(m + 1) * P])
            dve.wait_ge(gains_in, 48)
            dve.wait_ge(sincos_set, 1)

            front(0, 1, lambda c: None)
            boundary()
            with dve.Fori(1, BLOCKS) as b:
                front(b, BLOCKS, lambda c: steps(b - 1, c // 2, c % 2))
                stage(b - 1)
                boundary()
                finish(b - 1)
            with dve.Fori(0, CUTS // 2) as r:
                for par in range(2):
                    steps(BLOCKS - 1, r, par)
            dve.wait_ge(out_stored, 16 * (BLOCKS - 1))
            stage(BLOCKS - 1)
            finish(BLOCKS - 1)


def _chunks(m, halves, cols):
    return m.reshape(2, 4, P, halves, cols).transpose(3, 0, 2, 1, 4).reshape(2 * halves, P, 4 * cols)


def kernel(**inputs):
    import numpy as np
    import concourse.bacc as bacc
    from concourse.bass_utils import run_bass_kernel_spmd as run

    g = {k: np.asarray(v) for k, v in inputs.items()}
    one = {k: v[0] for k, v in g.items() if k != "g_final"}
    w_in = one["w_in"]
    at = np.cumsum([0, QRANK, KVRANK + ROPE, CONV, CONV, CONV])
    gate_b, gate_c, hx = (w_in[:, at[i]:at[i + 1]] for i in (2, 3, 4))
    arrays = {
        "x": one["x"], "mem": one["mem"],
        "pos": one["positions"].reshape(BLOCKS, P).T,
        "inv_freq": (np.float32(10000.0) ** (-np.arange(0, ROPE, 2, dtype=np.float32) / np.float32(ROPE)))[None],
        "gcol": np.concatenate([one[k].reshape(-1, P).T for k in ("g_mix", "g_q", "g_kv", "g_out", "g_x", "g_mem")], 1),
        "g_ffn": one["g_ffn"][None], "g_final": g["g_final"][None],
        "conv_w": one["conv_w"].reshape(1, TAPS * CONV),
        "w_cq": _chunks(w_in[:, at[0]:at[1]], 1, QRANK),
        "w_ckvr": _chunks(w_in[:, at[1]:at[2]], 1, KVRANK + ROPE),
        "w_conv": np.concatenate([_chunks(m, 1, CONV) for m in (gate_c, hx, gate_b)]),
        "w_uq": one["w_uq"].reshape(QT, P, 2, QRANK).transpose(2, 1, 0, 3).reshape(2, P, QT * QRANK),
        "w_ukv": one["w_ukv"].reshape(KVT, P, D).transpose(1, 0, 2).reshape(1, P, KVT * D),
        "w_o": _chunks(one["w_o"], 2, HALFC),
        "w_pq": _chunks(one["w_pq"], 2, HALFC),
        "keys": one["sub_keys"].transpose(1, 3, 0, 2).reshape(1, P, PHEADS * PKEYS),
        "w_xkv": _chunks(one["w_xkv"], 4, HALFC),
        "w_xqT": one["w_xq"].T.reshape(XHEADS, 2, P, D).transpose(0, 2, 1, 3).reshape(XHEADS, P, 2 * D),
        "w_xo": one["w_xo"].reshape(XHEADS, 2, P, D).transpose(0, 2, 1, 3).reshape(XHEADS, P, 2 * D),
        "experts": np.concatenate([one["u_experts"], one["v_experts"]], axis=1),
    }
    arrays = {k: np.ascontiguousarray(v) for k, v in arrays.items()}
    nc = bacc.Bacc("TRN2", target_bir_lowering=False, num_devices=1)
    w = {k: nc.dram_tensor("in_" + k, a.shape, mybir.dt.from_np(a.dtype), kind="ExternalInput").ap() for k, a in arrays.items()}
    for name in ("cross_a", "cross_b"):
        w[name] = nc.dram_tensor(name, [4, P, WCHUNK], F32, kind="Internal").ap()
    out = nc.dram_tensor("out", [1, SEQ, D], F32, kind="ExternalOutput").ap()
    layer_kernel(nc, w, out[0])
    return run(nc, [{"in_" + k: a for k, a in arrays.items()}], core_ids=[0]).results[0]["out"]
```

```python
import math
from contextlib import ExitStack

import concourse.bass as bass
from concourse import mybir

F32 = mybir.dt.float32
BF16 = mybir.dt.bfloat16
U32 = mybir.dt.uint32
I32 = mybir.dt.int32
ALU = mybir.AluOpType
ACT = mybir.ActivationFunctionType
AX_X = mybir.AxisListType.X

P = 128
SEQ = 1024
D = 1024
KT = D // P
BLOCKS = SEQ // P
MEM = 256
HEADS = 8
NOPE, ROPE, VDIM = 64, 32, 64
HALF = ROPE // 2
QK = NOPE + ROPE
QRANK, KVRANK = 384, 256
QT, KVT = QRANK // P, KVRANK // P
CONV = 512
TAPS = 3
GROUPS, GDIM = 16, 64
XHEADS, XDIM = 4, 256
PHEADS, PKEYS, PDIM = 8, 128, 64
TOPK = 16
EXPERTS = PHEADS * TOPK
EPS = 1e-6
NEG = -1e30
LOWEST = -3e38
ROUNDER = 1.5 * 2 ** 23
TURN_PARTS = (6.28125, 0.0019350051879882812, 2 * math.pi - 6.28125 - 0.0019350051879882812)
PI_BELOW = 3.1415925
HALFC = 512

RING = 8
STEPS_A_CUT = 4
CUTS = EXPERTS // STEPS_A_CUT
IDX_RING = 16
WRING = 3
WCHUNK = 2048
DIAGS = 4

LOOPS = [(1, BLOCKS // 2), (BLOCKS // 2, BLOCKS)]

HEAD_TURNS = [(0, 1), (2,), (3, 4), (5,), (6,), (7, 8, 9)]
AFTER = 7 + len(HEAD_TURNS)
TOPK_AT = AFTER + 10
CHOSEN_AT = TOPK_AT + 7

RECTS = [(0, 1, 16), (1, 1, 8), (2, 2, 5), (4, 4, 3), (8, 8, 1)]
CAND = sum(ni * nj for _, ni, nj in RECTS)

MIX, LORA, MIXED, CROSS, PROBS, FFN, PEERQ = range(7)
TURNS = 7
MEM_TURNS = 2
R_MIX, R_LORA, R_GROUP, R_CROSS, R_FFN = range(5)
ROOTS = 5
MEM_ROOTS = 2
POOL_CONSTS = 15
PRE_CHUNKS = 16
G_MIX, G_Q, G_KV, G_OUT, G_X, G_MEM = 0, KT, KT + QT, KT + QT + KVT, 2 * KT + QT + KVT, 3 * KT + QT + KVT
G_COLS = 4 * KT + QT + KVT


def block_chunks(w):
    return ([(w["w_cq"], c, 4 * QRANK) for c in range(2)]
            + [(w["w_ckvr"], c, 4 * (KVRANK + ROPE)) for c in range(2)]
            + [(w["w_conv"], c, WCHUNK) for c in range(6)]
            + [(w["w_uq"], c, QT * QRANK) for c in range(2)]
            + [(w["w_ukv"], 0, KVT * D)]
            + [(w["w_o"], c, WCHUNK) for c in range(4)]
            + [(w["cross_a"], c, WCHUNK) for c in range(4)]
            + [(w["cross_b"], c, WCHUNK) for c in range(4)]
            + [(w["w_pq"], c, WCHUNK) for c in range(4)]
            + [(w["keys"], 0, PHEADS * PKEYS)])


C_CQ, C_CKVR, C_CONV, C_UQ, C_UKV, C_O, C_A, C_B, C_PQ, C_KEYS = 0, 2, 4, 10, 12, 13, 17, 21, 25, 29
CHUNKS = 30
assert CHUNKS % WRING == 0

FOLDS = {0: ("kv", 0), 1: ("kv", 1), 2: ("a", 0), 4: ("a", 1), 7: ("kv", 2), 9: ("kv", 3),
         11: ("b", 0), AFTER: ("b", 1)}
PIECE_CHUNKS = {1: 4, 2: 4, 3: 2, 4: 3, AFTER + 1: 4, AFTER + 3: 4, AFTER + 5: 4, AFTER + 7: 4, AFTER + 9: 1}


def first_order():
    order, c = [], 0
    for piece in range(CUTS):
        if piece in FOLDS:
            order += [(*FOLDS[piece], q) for q in range(2)]
        for _ in range(PIECE_CHUNKS.get(piece, 0)):
            order.append(("front", 0, c))
            c += 1
    assert c == CHUNKS and len(order) == CHUNKS + PRE_CHUNKS
    return order


FIRST_ORDER = first_order()
FOLD_UNITS = [FOLDS[piece] for piece in sorted(FOLDS)]
BANKS = {u: sum(2 if v[0] == "kv" else 8 for v in FOLD_UNITS[:i + 1]) for i, u in enumerate(FOLD_UNITS)}


def layer_kernel(nc, w, out):
    ctx = ExitStack()
    with ctx:
        def sb(name, shape, dt=F32):
            return ctx.enter_context(nc.sbuf_tensor(name, shape, dt))

        def pb(name, shape):
            return ctx.enter_context(nc.psum_tensor(name, shape, F32))

        def sem(name):
            return ctx.enter_context(nc.semaphore(name))

        rows = sb("rows", [P, RING, 2 * D])
        wbuf = sb("wbuf", [P, WRING, WCHUNK])
        kT = sb("kT", [QK, HEADS, SEQ])
        vals = sb("vals", [P, BLOCKS, HEADS * VDIM])
        big = sb("big", [P, 2, D])
        big2 = sb("big2", [P, 2, D])
        h = sb("h", [P, D])
        tile = sb("tile", [P, D])
        turned = sb("turned", [P, D])
        hn = sb("hn", [P, D])
        g_ffn = sb("g_ffn_b", [P, D])
        g_fin = sb("g_fin_b", [P, D])
        convw = sb("convw", [P, TAPS, CONV])
        tail = sb("tail", [P, 2, CONV])
        qk = sb("qk", [P, 2 * HEADS, QK])
        tri = sb("tri", [P, SEQ + (BLOCKS - 1) * P], BF16)
        diag = sb("diag", [P, DIAGS, P])
        ident = sb("ident", [P, P])
        shift = sb("shift", [P, 2, P])
        carry = sb("carry", [P, 2, P])
        gcol = sb("gcol", [P, G_COLS])
        cos_t = sb("cos_t", [P, BLOCKS, HALF])
        sin_t = sb("sin_t", [P, BLOCKS, HALF])
        best_v = sb("best_v", [P, 2 * PHEADS, TOPK])
        best_i = sb("best_i", [P, 2 * PHEADS, TOPK], U32)
        best_f = sb("best_f", [P, 2 * PHEADS, TOPK])
        gates_next = sb("gates_next", [P, EXPERTS])
        gates = sb("gates", [P, EXPERTS])
        idx_next = sb("idx_next", [P, EXPERTS], U32)
        idx_cur = sb("idx_cur", [P, EXPERTS], U32)
        idx_ring = sb("idx_ring", [P, IDX_RING], U32)
        iota_c = sb("iota_c", [P, CAND])
        ss = sb("ss", [P, 40])
        std = sb("std", [P, 40])
        rinv = sb("rinv", [P, 40])
        mx = sb("mx", [P, HEADS])
        nmx = sb("nmx", [P, HEADS])
        rsum = sb("rsum", [P, HEADS])
        eps = sb("eps", [P, 1])
        dot = sb("dot", [P, RING])
        act_v = sb("act_v", [P, RING])
        act_g = sb("act_g", [P, RING])

        acc = pb("acc", [P, D])
        pT = pb("pT", [P, D])
        pM = pb("pM", [P, D])
        pS = pb("pS", [P, D])

        gate_c = big2[:, 0, 0:CONV]
        z = big2[:, 0, CONV:2 * CONV]
        lora = big2[:, 1, 0:QRANK + KVRANK + ROPE]
        taps = big[:].rearrange("p a d -> p (a d)")[:, 0:TAPS * CONV].rearrange("p (k d) -> p k d", k=TAPS)
        gate_b = big[:, 1, CONV:]
        rtmp = big2[:, 0, 0:4 * HEADS * HALF].rearrange("p (k h f) -> p k h f", k=2, h=2 * HEADS)
        top_p = best_i[:, 0:PHEADS, :]
        top_f = best_v[:, PHEADS:, :]
        top_m = best_v[:, 0:PHEADS, :]
        pscore = big[:].rearrange("p a d -> p (a d)").rearrange("p (s n) -> p s n", s=2 * PHEADS)
        rest = big2[:, 0, :].rearrange("p (s n) -> p s n", s=8)
        qk_flat = qk[:].rearrange("p a d -> p (a d)")
        cand_v = qk_flat[:, 0:PHEADS * CAND].rearrange("p (h c) -> p h c", h=PHEADS)
        cand_i = qk_flat[:, PHEADS * CAND:2 * PHEADS * CAND].rearrange("p (h c) -> p h c", h=PHEADS)
        cand_r = qk_flat[:, 2 * PHEADS * CAND:3 * PHEADS * CAND].rearrange("p (h c) -> p h c", h=PHEADS)
        top_v = qk_flat[:, 3 * PHEADS * CAND:3 * PHEADS * CAND + EXPERTS].rearrange("p (h k) -> p h k", h=PHEADS)
        hit = [big2[:, s, 0:TOPK * CAND].rearrange("p (k c) -> p k c", k=TOPK) for s in range(2)]
        qT = turned[0:QK, :].rearrange("p (h t) -> p h t", h=HEADS)
        turned3 = turned[:].rearrange("p (k t) -> p k t", k=KT)
        pT3 = pT[:].rearrange("p (k t) -> p k t", k=KT)
        pS3 = pS[:].rearrange("p (k t) -> p k t", k=KT)
        out_stage = big2[:, 1, :]
        memT = rows[:, 0, :].rearrange("p (k m) -> p k m", k=KT)
        xkT = rows[:, 1, :].rearrange("p (k m) -> p k m", k=KT)
        xvT = rows[:, 2, :].rearrange("p (k m) -> p k m", k=KT)
        fold = [rows[:, 3 + s, :].rearrange("p (k m) -> p k m", k=4) for s in range(2)]
        memx = rows[:, 5:7, 0:D]
        ang = rows[:, 7, 0:4 * P].rearrange("p (k b f) -> p k b f", k=4, b=BLOCKS)
        posf = rows[:, 7, 4 * P:4 * P + BLOCKS]
        invf = rows[:, 7, 5 * P:5 * P + HALF]
        posi = rows[:, 7, 6 * P:6 * P + BLOCKS].bitcast(I32)

        consts_in = sem("consts_in")
        gains_in = sem("gains_in")
        mem_in = sem("mem_in")
        x_in = sem("x_in")
        w_in = [sem(f"w_in{i}") for i in range(WRING)]
        w_done = sem("w_done")
        pool_set = sem("pool_set")
        angle_set = sem("angle_set")
        sincos_set = sem("sincos_set")
        dve_set = sem("dve_set")
        root_set = sem("root_set")
        tile_set = sem("tile_set")
        turn_set = sem("turn_set")
        turned_set = sem("turned_set")
        fold_set = sem("fold_set")
        fold_out = sem("fold_out")
        fold_stored = [sem(f"fold_stored{s}") for s in range(2)]
        in_out = sem("in_out")
        z_set = sem("z_set")
        taps_set = sem("taps_set")
        conv_set = sem("conv_set")
        conv_out = sem("conv_out")
        tail_set = sem("tail_set")
        q_out = sem("q_out")
        kv_out = sem("kv_out")
        v_out = sem("v_out")
        qk_set = sem("qk_set")
        qk_turn = sem("qk_turn")
        qT_set = sem("qT_set")
        kT_set = sem("kT_set")
        score_set = sem("score_set")
        masked_set = sem("masked_set")
        prob_set = sem("prob_set")
        prob_turn = sem("prob_turn")
        probT_set = sem("probT_set")
        head_out = sem("head_out")
        gsum_set = sem("gsum_set")
        h_mix = sem("h_mix")
        xmax_set = sem("xmax_set")
        xexp_set = sem("xexp_set")
        h_cross = sem("h_cross")
        pscore_out = sem("pscore_out")
        gate_in = sem("gate_in")
        gate_exp = sem("gate_exp")
        chosen = sem("chosen")
        idx_taken = sem("idx_taken")
        gates_taken = sem("gates_taken")
        hn_taken = sem("hn_taken")
        h_taken = sem("h_taken")
        pool_past = sem("pool_past")
        sp_past = sem("sp_past")
        dve_past = sem("dve_past")
        idx_staged = sem("idx_staged")
        rows_in = [sem(f"rows_in{i}") for i in range(RING)]
        ring_open = sem("ring_open")
        dot_set = sem("dot_set")
        diag_set = sem("diag_set")
        acc_out = sem("acc_out")
        final_root = sem("final_root")
        out_set = sem("out_set")
        out_stored = sem("out_stored")

        block = ctx.enter_context(nc.Block())

        def turn_no(b, stage):
            return b * TURNS + MEM_TURNS + stage + 1

        def root_no(b, stage):
            return b * ROOTS + MEM_ROOTS + stage + 1

        def chunk_no(b, c):
            return FIRST_ORDER.index(("front", 0, c)) if isinstance(b, int) else PRE_CHUNKS + c

        def chunk_slot(b, c):
            return chunk_no(b, c) % WRING

        def chunk_in(eng, b, c):
            eng.wait_ge(w_in[chunk_slot(b, c)],
                        b * (16 * CHUNKS // WRING) + 16 * (chunk_no(b, c) // WRING + 1))

        def multiplied(eng, b, c):
            eng.wait_ge(w_done, b * CHUNKS + chunk_no(b, c) + 1)

        def fold_no(unit, q):
            return FIRST_ORDER.index((*unit, q))

        def fold_chunk_in(eng, unit, q):
            no = fold_no(unit, q)
            eng.wait_ge(w_in[no % WRING], 16 * (no // WRING + 1))

        @block.sync
        def _(sp):
            for name, dst in (("gcol", gcol[:]), ("pos", posi)):
                sp.dma_start(dst, w[name]).then_inc(consts_in, 16)
            sp.dma_start(invf, w["inv_freq"].to_broadcast([P, HALF])).then_inc(consts_in, 16)
            sp.dma_start(memx, w["mem"].rearrange("(m p) d -> p m d", p=P)).then_inc(mem_in, 16)

            sp.dma_start(h[:], w["x"][0:P, :]).then_inc(x_in, 16)
            folds = {"kv": w["w_xkv"], "a": w["w_xqT"], "b": w["w_xo"]}
            for no, (kind, part, c) in enumerate(FIRST_ORDER):
                if kind == "front":
                    src, k, cols = block_chunks(w)[c]
                    src = src[k]
                else:
                    src, cols = folds[kind][2 * part + c], WCHUNK
                if (kind, c) in (("front", C_A), ("front", C_B)):
                    for s in range(2):
                        sp.wait_ge(fold_stored[s], 16 * (2 if c == C_A else 4))
                if no >= WRING:
                    sp.wait_ge(w_done, no - WRING + 1)
                sp.dma_start(wbuf[:, no % WRING, 0:cols], src).then_inc(w_in[no % WRING], 16)
                if no == WRING - 1:
                    sp.dma_start(g_ffn[:], w["g_ffn"].to_broadcast([P, D])).then_inc(gains_in, 16)
                    sp.dma_start(g_fin[:], w["g_final"].to_broadcast([P, D])).then_inc(gains_in, 16)
                    sp.dma_start(convw[:].rearrange("p k d -> p (k d)"), w["conv_w"].to_broadcast([P, TAPS * CONV]))\
                        .then_inc(gains_in, 16)

            def loads(b):
                sp.wait_ge(h_taken, b)
                sp.dma_start(h[:], w["x"][bass.ds(b * P, P), :]).then_inc(x_in, 16)
                for c, (src, k, cols) in enumerate(block_chunks(w)):
                    sp.wait_ge(w_done, b * CHUNKS + PRE_CHUNKS + c - WRING + 1)
                    sp.dma_start(wbuf[:, chunk_slot(b, c), 0:cols], src[k]).then_inc(w_in[chunk_slot(b, c)], 16)

            def store(b):
                sp.wait_ge(out_set, b + 1)
                sp.dma_start(out[bass.ds(b * P, P), :], out_stage).then_inc(out_stored, 16)
                sp.wait_ge(out_stored, b * 16 + 16)
                sp.sem_inc(sp_past, 1)

            with sp.Fori(1, BLOCKS) as b:
                loads(b)
                store(b - 1)
            store(BLOCKS - 1)
            for s in range(2):
                sp.wait_ge(fold_stored[s], 16 * 4)

        @block.gpsimd
        def _(pool):
            done = [0]

            def made(ins):
                done[0] += 1
                ins.then_inc(pool_set, 1)

            made(pool.memset(ident[:], 0.0))
            pool.wait_ge(pool_set, 1)
            made(pool.affine_select(out=ident[:], in_=ident[:], compare_op=ALU.not_equal, fill=1.0, base=0,
                                    pattern=[[-1, P]], channel_multiplier=1))
            made(pool.memset(shift[:], 0.0))
            made(pool.memset(carry[:], 0.0))
            made(pool.memset(tri[:], 0.0))
            pool.wait_ge(pool_set, done[0])
            for k in range(2):
                made(pool.affine_select(out=shift[:, k, :], in_=shift[:, k, :], compare_op=ALU.not_equal, fill=1.0,
                                        base=1 + k, pattern=[[-1, P]], channel_multiplier=1))
                made(pool.affine_select(out=carry[:, k, :], in_=carry[:, k, :], compare_op=ALU.not_equal, fill=1.0,
                                        base=1 + k - P, pattern=[[-1, P]], channel_multiplier=1))
            made(pool.affine_select(out=tri[:], in_=tri[:], compare_op=ALU.is_ge, fill=NEG, base=(BLOCKS - 1) * P,
                                    pattern=[[-1, SEQ + (BLOCKS - 1) * P]], channel_multiplier=1))
            made(pool.iota(idx_next[:, 0:CAND], pattern=[[1, CAND]], base=0, channel_multiplier=0))
            pool.wait_ge(pool_set, done[0])
            made(pool.tensor_copy(iota_c[:], idx_next[:, 0:CAND]))
            made(pool.memset(tail[:], 0.0))
            made(pool.memset(kT[:], 0.0))
            made(pool.memset(vals[:], 0.0))
            assert done[0] == POOL_CONSTS

            with pool.Fori(0, BLOCKS) as b:
                pool.wait_ge(chosen, b + 1)
                pool.sem_inc(pool_past, 1)
                pool.tensor_copy(idx_cur[:], idx_next[:]).then_inc(idx_taken, 1)
                pool.wait_ge(idx_taken, b + 1)
                pool.sem_inc(pool_past, 1)
                with pool.Fori(0, EXPERTS // IDX_RING) as r:
                    for g in range(IDX_RING // 4):
                        cols = slice(4 * g, 4 * g + 4)
                        pool.tensor_copy(idx_ring[:, cols], idx_cur[:, bass.ds(r * IDX_RING + 4 * g, 4)])\
                            .then_inc(idx_staged, 1)
                        pool.wait_ge(idx_staged, b * (EXPERTS // 4) + r * (IDX_RING // 4) + g + 1)
                        for k in range(4 * g, 4 * g + 4):
                            pool.wait_ge(ring_open, b * EXPERTS + r * IDX_RING + k + 1)
                            pool.sem_inc(pool_past, 1)
                            pool.indirect_dma_start(
                                out=rows[:, k % RING, :], out_offset=None, in_=w["experts"][:, :],
                                in_offset=bass.IndirectOffsetOnAxis(ap=idx_ring[:, k:k + 1], axis=0),
                            ).then_inc(rows_in[k % RING], 16)
        @block.scalar
        def _(act):
            def steps(b, rnd, par):
                first = par * STEPS_A_CUT
                slots = range(first, first + STEPS_A_CUT)
                n = b * EXPERTS + rnd * RING + first
                act.wait_ge(dot_set, n + STEPS_A_CUT)
                act.activation(act_v[:, first:first + STEPS_A_CUT], dot[:, first:first + STEPS_A_CUT],
                               ACT.Gelu_apprx_tanh)
                act.drain()
                for s in slots:
                    act.activation(act_g[:, s:s + 1], gates[:, bass.ds(rnd * RING + s, 1)], ACT.Copy,
                                   scale=act_v[:, s:s + 1])
                act.drain()
                act.wait_ge(ring_open, n + STEPS_A_CUT + RING - DIAGS)
                for s in slots:
                    act.activation(diag[:, s % DIAGS, :], ident[:], ACT.Copy, scale=act_g[:, s:s + 1])\
                        .then_inc(diag_set, 1)

            def root(src, col, width, n=1, junk=None):
                act.activation(junk, src, ACT.Square, accum_out=ss[:, col:col + n])

            def roots(col, n, width):
                act.drain()
                return act.activation(std[:, col:col + n], ss[:, col:col + n], ACT.Sqrt, bias=eps[:, 0:1],
                                      scale=1.0 / width)

            def front(b, keys, cut):
                cut(0)
                act.wait_ge(x_in, b * 16 + 16)
                if keys > 1:
                    act.wait_ge(hn_taken, b)
                root(h[:], 0, D, junk=tile[:])
                roots(0, 1, D).then_inc(root_set, 1)
                cut(1)
                cut(2)
                multiplied(act, b, C_CQ + 1)
                act.copy(lora[:, 0:QRANK], pM[:, 0:QRANK]).then_inc(in_out, 1)
                multiplied(act, b, C_CQ + 3)
                act.copy(lora[:, QRANK:], pM[:, HALFC:HALFC + KVRANK + ROPE]).then_inc(in_out, 1)
                act.drain()
                root(lora[:, 0:QRANK], 1, QRANK, junk=tile[:, 0:QRANK])
                root(lora[:, QRANK:QRANK + KVRANK], 2, KVRANK, junk=tile[:, QRANK:QRANK + KVRANK])
                roots(1, 1, QRANK)
                act.activation(std[:, 2:3], ss[:, 2:3], ACT.Sqrt, bias=eps[:, 0:1], scale=1.0 / KVRANK)\
                    .then_inc(root_set, 1)
                cut(3)
                multiplied(act, b, C_CONV + 1)
                act.copy(gate_c, pM[:, 0:HALFC]).then_inc(in_out, 1)
                cut(4)
                multiplied(act, b, C_CONV + 5)
                act.copy(gate_b, pM[:, 0:HALFC]).then_inc(in_out, 1)
                cut(5)
                multiplied(act, b, C_UQ + 1)
                act.copy(qk[:, 0:4, :], pM[:, 0:QRANK].rearrange("p (h d) -> p h d", h=4))
                act.copy(qk[:, 4:8, :], pM[:, HALFC:HALFC + QRANK].rearrange("p (h d) -> p h d", h=4))\
                    .then_inc(q_out, 1)
                multiplied(act, b, C_UKV)
                act.wait_ge(v_out, b + 1)
                kv = pS[:].rearrange("p (h d) -> p h d", h=HEADS)
                act.copy(qk[:, HEADS:, 0:NOPE], kv[:, :, 0:NOPE]).then_inc(kv_out, 1)
                cut(6)
                act.wait_ge(conv_set, b + 1)
                act.copy(tail[:], taps[:, 0:2, :]).then_inc(tail_set, 1)
                act.wait_ge(qk_turn, b * 2 + 1)
                act.copy(qT, pT3[0:QK, :, :]).then_inc(qT_set, 1)

                def exps(hd):
                    act.wait_ge(masked_set, b * HEADS + hd + 1)
                    act.activation(big[:, hd % 2, 0:keys * P], big[:, hd % 2, 0:keys * P], ACT.Exp,
                                   bias=nmx[:, hd:hd + 1], scale=1.0 / math.sqrt(QK),
                                   accum_out=rsum[:, hd:hd + 1]).then_inc(prob_set, 1)

                def probT(hd):
                    act.wait_ge(prob_turn, b * HEADS + hd + 1)
                    if hd >= 2:
                        act.wait_ge(head_out, b * HEADS + hd - 1)
                    act.copy(big2[:, hd % 2, 0:keys * P], pT[:, 0:keys * P]).then_inc(probT_set, 1)

                for c, its in enumerate(HEAD_TURNS):
                    cut(7 + c)
                    for it in its:
                        if 1 <= it <= HEADS:
                            probT(it - 1)
                        if it < HEADS:
                            exps(it)
                cut(AFTER)
                act.wait_ge(gsum_set, b + 1)
                act.activation(std[:, 8:8 + GROUPS], ss[:, 8:8 + GROUPS], ACT.Sqrt, bias=eps[:, 0:1],
                               scale=1.0 / GDIM).then_inc(root_set, 1)
                cut(AFTER + 1)
                cut(AFTER + 2)
                act.wait_ge(h_mix, b * 2 + 2)
                root(h[:], 3, D, junk=tile[:])
                roots(3, 1, D).then_inc(root_set, 1)
                cut(AFTER + 3)
                cut(AFTER + 4)
                act.wait_ge(xmax_set, b + 1)
                for hd in range(XHEADS):
                    ins = act.activation(tile[:, hd * MEM:(hd + 1) * MEM], pM[:, hd * MEM:(hd + 1) * MEM], ACT.Exp,
                                         bias=nmx[:, hd:hd + 1], scale=1.0 / math.sqrt(XDIM),
                                         accum_out=rsum[:, hd:hd + 1])
                ins.then_inc(xexp_set, 1)
                cut(AFTER + 5)
                cut(AFTER + 6)
                act.wait_ge(h_cross, b * 2 + 2)
                root(h[:], 4, D, junk=big[:, 0, :])
                roots(4, 1, D).then_inc(root_set, 1)
                cut(AFTER + 7)
                cut(AFTER + 8)
                multiplied(act, b, C_PQ + 3)
                act.copy(big[:, 1, :], pM[:]).then_inc(tile_set, 1)
                cut(AFTER + 9)
                cut(TOPK_AT)
                multiplied(act, b, C_KEYS)
                flat = big[:].rearrange("p a d -> p (a d)")
                act.copy(flat[:, 0:D], pS[:])
                act.copy(flat[:, D:2 * D], pM[:]).then_inc(pscore_out, 1)
                for c in range(TOPK_AT + 1, CHOSEN_AT + 1):
                    cut(c)
                act.wait_ge(gate_in, b + 1)
                act.activation(top_f, top_m, ACT.Exp).then_inc(gate_exp, 1)
                for c in range(CHOSEN_AT + 1, CUTS):
                    cut(c)

            def boundary(b):
                act.wait_ge(chosen, b + 1)
                act.copy(gates[:], gates_next[:]).then_inc(gates_taken, 1)
                act.drain()

            def finish(b):
                act.wait_ge(acc_out, b + 1)
                root(out_stage, 5, D, junk=big2[:, 0, :])
                roots(5, 1, D).then_inc(final_root, 1)

            def folds(piece):
                if 7 <= piece < AFTER:
                    piece -= 1
                if piece not in FOLDS:
                    return
                unit = FOLDS[piece]
                kind, part = unit
                last = fold_no(unit, 1) + 1
                if kind == "kv":
                    dst = (xkT, xvT)[part // 2]
                    act.wait_ge(w_done, last)
                    for half in range(2):
                        at = 4 * (part % 2) + 2 * half
                        act.copy(dst[:, at:at + 2, :], acc[:, half * HALFC:(half + 1) * HALFC]
                                 .rearrange("p (k m) -> p k m", k=2)).then_inc(fold_out, 1)
                    return
                for q in range(2):
                    stage = 2 * (part if kind == "a" else 2 + part) + q
                    c = 2 * part + q if kind == "a" else 2 * q + part
                    if stage >= 2:
                        act.wait_ge(fold_stored[q], 16 * (stage // 2))
                    for k in range(4):
                        if q == 1 and k == 3:
                            act.wait_ge(w_done, last)
                        else:
                            act.wait_ge(fold_set, stage * 4 + k + 1 - stage // 2)
                        act.copy(fold[q][:, k, :], acc[:, k % 2 * HALFC:(k % 2 + 1) * HALFC]).then_inc(fold_out, 1)
                    act.wait_ge(fold_out, BANKS[unit] - 4 * (1 - q))
                    act.dma_start(w["cross_" + kind][c], rows[:, 3 + q, :]).then_inc(fold_stored[q], 16)

            act.wait_ge(dve_set, 1)
            act.wait_ge(angle_set, 1)
            act.activation(sin_t[:], ang[:, 2], ACT.Sin)
            act.activation(cos_t[:], ang[:, 3], ACT.Sin).then_inc(sincos_set, 1)
            act.wait_ge(mem_in, 16)
            for m in range(2):
                if m == 1:
                    act.wait_ge(turn_set, 1)
                root(memx[:, m, :], 6 + m, D, junk=tile[:])
                roots(6 + m, 1, D).then_inc(root_set, 1)
            act.wait_ge(pool_set, POOL_CONSTS)
            act.wait_ge(turn_set, MEM_TURNS)
            front(0, 1, folds)
            boundary(0)
            for first, last in LOOPS:
                with act.Fori(first, last) as b:
                    front(b, last, lambda c: steps(b - 1, c // 2, c % 2))
                    boundary(b)
                    finish(b - 1)
            with act.Fori(0, CUTS // 2) as r:
                for par in range(2):
                    steps(BLOCKS - 1, r, par)
            finish(BLOCKS - 1)


        @block.tensor
        def _(pe):
            def steps(b, rnd, par):
                for i in range(STEPS_A_CUT):
                    s = par * STEPS_A_CUT + i
                    pe.wait_ge(diag_set, b * EXPERTS + rnd * RING + s + 1)
                    for half in range(2):
                        cols = slice(half * HALFC, (half + 1) * HALFC)
                        mm = pe.matmul(acc[:, cols], diag[:, s % DIAGS, :],
                                       rows[:, s, D + half * HALFC:D + (half + 1) * HALFC],
                                       start=False, stop=False, skip_group_check=True)
                    mm.then_inc(ring_open, 1)

            def turn(src, b, stage, tiles=KT):
                pe.wait_ge(tile_set, turn_no(b, stage))
                for k in range(tiles):
                    tr = pe.transpose(pT3[:, k, :], src[:, k * P:(k + 1) * P], ident[:])
                tr.then_inc(turn_set, 1)

            def project(b, c, half, first_tile=0, width=HALFC, bank=None):
                bank = half if bank is None else bank
                for q in range(2):
                    chunk_in(pe, b, c + q)
                    for k in range(4):
                        mm = pe.matmul(pM[:, bank * HALFC:bank * HALFC + width], turned3[:, 4 * q + k, :],
                                       wbuf[:, chunk_slot(b, c + q), k * width:(k + 1) * width],
                                       start=(q == 0 and k == 0), stop=(q == 1 and k == 3))
                    mm.then_inc(w_done, 1)
                return mm

            def front(b, keys, cut):
                cut(0)
                turn(tile[:], b, MIX)
                cut(1)
                pe.wait_ge(turned_set, turn_no(b, MIX))
                project(b, C_CQ, 0, width=QRANK, bank=0)
                project(b, C_CQ + 2, 0, width=KVRANK + ROPE, bank=1)
                cut(2)
                pe.wait_ge(in_out, b * 4 + 1)
                project(b, C_CONV, 0, bank=0)
                pe.wait_ge(in_out, b * 4 + 2)
                project(b, C_CONV + 2, 0, bank=1)
                cut(3)
                pe.wait_ge(in_out, b * 4 + 3)
                project(b, C_CONV + 4, 0, bank=0)
                turn(tile[:], b, LORA, QT + KVT)
                cut(4)
                pe.wait_ge(turned_set, turn_no(b, LORA))
                pe.wait_ge(in_out, b * 4 + 4)
                pe.wait_ge(z_set, b + 1)
                for half in range(2):
                    chunk_in(pe, b, C_UQ + half)
                    for k in range(QT):
                        mm = pe.matmul(pM[:, half * HALFC:half * HALFC + QRANK], turned3[:, k, :],
                                       wbuf[:, chunk_slot(b, C_UQ + half), k * QRANK:(k + 1) * QRANK],
                                       start=(k == 0), stop=(k == QT - 1))
                    mm.then_inc(w_done, 1)
                chunk_in(pe, b, C_UKV)
                for half in range(2):
                    for k in range(KVT):
                        mm = pe.matmul(pS[:, half * HALFC:(half + 1) * HALFC], turned3[:, QT + k, :],
                                       wbuf[:, chunk_slot(b, C_UKV), k * D + half * HALFC:k * D + (half + 1) * HALFC],
                                       start=(k == 0), stop=(k == KVT - 1))
                mm.then_inc(w_done, 1)
                cut(5)
                pe.wait_ge(q_out, b + 1)
                pe.wait_ge(taps_set, b + 1)
                if keys > 1:
                    pe.wait_ge(tail_set, b)
                pe.matmul(pM[:, 0:CONV], ident[:], taps[:, 2, :], start=True, stop=False)
                for k in range(2):
                    pe.matmul(pM[:, 0:CONV], shift[:, k, :], taps[:, 1 - k, :], start=False, stop=False)
                    mm = pe.matmul(pM[:, 0:CONV], carry[:, k, :], tail[:, 1 - k, :], start=False, stop=(k == 1))
                mm.then_inc(conv_set, 1)
                pe.wait_ge(qk_set, b + 1)
                for hd in range(HEADS):
                    tr = pe.transpose(pT3[0:QK, hd, :], qk[:, hd, :], ident[:])
                tr.then_inc(qk_turn, 1)
                pe.wait_ge(kv_out, b + 1)
                for hd in range(HEADS):
                    tr = pe.transpose(pS3[0:QK, hd, :], qk[:, HEADS + hd, :], ident[:])
                tr.then_inc(qk_turn, 1)
                cut(6)
                pe.wait_ge(qT_set, b + 1)
                pe.wait_ge(kT_set, b + 1)
                pe.wait_ge(conv_out, b + 1)
                pe.wait_ge(v_out, b + 1)

                def scores(hd):
                    if hd:
                        pe.wait_ge(masked_set, b * HEADS + hd)
                    for c in range(0, keys * P, HALFC):
                        n = min(HALFC, keys * P)
                        mm = pe.matmul(pS[:, c:c + n], qT[:, hd, :], kT[:, hd, c:c + n], start=True, stop=True)
                    mm.then_inc(score_set, 1)

                def turn_probs(hd):
                    pe.wait_ge(prob_set, b * HEADS + hd + 1)
                    if hd:
                        pe.wait_ge(probT_set, b * HEADS + hd)
                    for k in range(keys):
                        tr = pe.transpose(pT3[:, k, :], big[:, hd % 2, k * P:(k + 1) * P], ident[:])
                    tr.then_inc(prob_turn, 1)

                def weigh(hd):
                    pe.wait_ge(probT_set, b * HEADS + hd + 1)
                    for k in range(keys):
                        mm = pe.matmul(pM[:, hd * VDIM:(hd + 1) * VDIM], big2[:, hd % 2, k * P:(k + 1) * P],
                                       vals[:, k, hd * VDIM:(hd + 1) * VDIM], start=(k == 0), stop=(k == keys - 1))
                    mm.then_inc(head_out, 1)

                for c, its in enumerate(HEAD_TURNS):
                    for it in its:
                        if it < HEADS:
                            scores(it)
                        if 1 <= it <= HEADS:
                            turn_probs(it - 1)
                        if it >= 2:
                            weigh(it - 2)
                    cut(7 + c)
                cut(AFTER)
                turn(tile[:], b, MIXED)
                cut(AFTER + 1)
                pe.wait_ge(turned_set, turn_no(b, MIXED))
                for half in range(2):
                    project(b, C_O + 2 * half, half)
                cut(AFTER + 2)
                turn(tile[:], b, CROSS)
                cut(AFTER + 3)
                pe.wait_ge(turned_set, turn_no(b, CROSS))
                for half in range(2):
                    project(b, C_A + 2 * half, half)
                cut(AFTER + 4)
                turn(tile[:], b, PROBS)
                cut(AFTER + 5)
                pe.wait_ge(turned_set, turn_no(b, PROBS))
                for half in range(2):
                    project(b, C_B + 2 * half, half)
                cut(AFTER + 6)
                turn(tile[:], b, FFN)
                cut(AFTER + 7)
                pe.wait_ge(turned_set, turn_no(b, FFN))
                for half in range(2):
                    project(b, C_PQ + 2 * half, half)
                cut(AFTER + 8)
                turn(big[:, 1, :], b, PEERQ)
                cut(AFTER + 9)
                pe.wait_ge(turned_set, turn_no(b, PEERQ))
                chunk_in(pe, b, C_KEYS)
                for hc in range(2 * PHEADS):
                    hd, c = hc // 2, hc % 2
                    mm = pe.matmul((pS, pM)[c][:, hd * PKEYS:(hd + 1) * PKEYS], turned3[c * PDIM:(c + 1) * PDIM, hd, :],
                                   wbuf[c * PDIM:(c + 1) * PDIM, chunk_slot(b, C_KEYS), hd * PKEYS:(hd + 1) * PKEYS],
                                   start=True, stop=True)
                mm.then_inc(w_done, 1)
                for c in range(TOPK_AT, CUTS):
                    cut(c)

            def boundary(b, first):
                if not first:
                    pe.wait_ge(acc_out, b)
                pe.wait_ge(h_cross, 2 * b + 2)
                for half in range(2):
                    cols = slice(half * HALFC, (half + 1) * HALFC)
                    mm = pe.matmul(acc[:, cols], ident[:], h[:, cols], start=True, stop=False, skip_group_check=True)
                mm.then_inc(h_taken, 1)

            pe.sem_inc(ring_open, RING)
            pe.wait_ge(pool_set, 2)
            for m in range(2):
                pe.wait_ge(tile_set, m + 1)
                if m:
                    pe.wait_ge(turned_set, m)
                for k in range(KT):
                    tr = pe.transpose(pT3[:, k, :], tile[:, k * P:(k + 1) * P], ident[:])
                tr.then_inc(turn_set, 1)
            pe.wait_ge(turned_set, 2)
            pe.wait_ge(pool_set, POOL_CONSTS)

            def folds(piece):
                if piece not in FOLDS:
                    return
                unit = FOLDS[piece]
                kind, part = unit
                used = BANKS[unit] - (2 if kind == "kv" else 8)
                if kind == "kv":
                    if used:
                        pe.wait_ge(fold_out, used)
                    for q in range(2):
                        fold_chunk_in(pe, unit, q)
                    for ct in range(4):
                        for k in range(KT):
                            chunk = wbuf[:, fold_no(unit, k // 4) % WRING, :]
                            mm = pe.matmul(acc[:, ct * MEM:(ct + 1) * MEM],
                                           chunk[:, k % 4 * HALFC + ct * P:k % 4 * HALFC + (ct + 1) * P],
                                           memT[:, k, :], start=(k == 0), stop=(k == KT - 1))
                    mm.then_inc(w_done, 2)
                    return
                pe.wait_ge(fold_out, BANKS["kv", part + (0 if kind == "a" else 2)])
                for q in range(2):
                    fold_chunk_in(pe, unit, q)
                chunks = [wbuf[:, fold_no(unit, q) % WRING, :] for q in range(2)]
                for q in range(2):
                    for k in range(4):
                        pe.wait_ge(fold_out, used + 4 * q + k - 1)
                        bank = acc[:, k % 2 * HALFC:(k % 2 + 1) * HALFC]
                        if kind == "a":
                            for hh in range(2):
                                for dt in range(2):
                                    at = dt * D + (q * 4 + k) * P
                                    mm = pe.matmul(bank[:, hh * MEM:(hh + 1) * MEM], chunks[hh][:, at:at + P],
                                                   xkT[:, (2 * part + hh) * 2 + dt, :], start=(dt == 0), stop=(dt == 1))
                        else:
                            for dt in range(2):
                                at = dt * D + q * HALFC
                                mm = pe.matmul(bank, xvT[:, (2 * part + k // 2) * 2 + dt, k % 2 * P:(k % 2 + 1) * P],
                                               chunks[k // 2][:, at:at + HALFC], start=(dt == 0), stop=(dt == 1))
                        if q == 1 and k == 3:
                            mm.then_inc(w_done, 2)
                        else:
                            mm.then_inc(fold_set, 1)

            front(0, 1, folds)
            pe.wait_ge(fold_out, BANKS[FOLD_UNITS[-1]])
            boundary(0, True)
            for first, last in LOOPS:
                with pe.Fori(first, last) as b:
                    front(b, last, lambda c: steps(b - 1, c // 2, c % 2))
                    boundary(b, False)
            with pe.Fori(0, CUTS // 2) as r:
                for par in range(2):
                    steps(BLOCKS - 1, r, par)

        @block.vector
        def _(dve):
            def steps(b, rnd, par):
                for i in range(STEPS_A_CUT):
                    s = par * STEPS_A_CUT + i
                    dve.wait_ge(rows_in[s], b * (16 * EXPERTS // RING) + rnd * 16 + 16)
                    dve.tensor_tensor_reduce(out=rows[:, s, 0:D], in0=rows[:, s, 0:D], in1=hn[:], scale=1.0,
                                             scalar=0.0, op0=ALU.mult, op1=ALU.add,
                                             accum_out=dot[:, s:s + 1]).then_inc(dot_set, 1)

            def take_root(no, col, n=1):
                dve.wait_ge(root_set, no)
                dve.reciprocal(rinv[:, col:col + n], std[:, col:col + n])
                dve.drain()

            def out_of_turn(no, gain, tiles=KT, dst=None):
                dve.wait_ge(turn_set, no)
                dst = turned3[:, 0:tiles, :] if dst is None else dst
                if gain is None:
                    dve.tensor_copy(dst, pT3[:, 0:tiles, :]).then_inc(turned_set, 1)
                else:
                    g = gcol[:, gain:gain + tiles].unsqueeze(2).to_broadcast([P, tiles, P])
                    dve.tensor_tensor(dst, pT3[:, 0:tiles, :], g, ALU.mult).then_inc(turned_set, 1)

            def front(b, keys, cut):
                cut(0)
                take_root(root_no(b, R_MIX), 0)
                dve.tensor_scalar(tile[:], h[:], rinv[:, 0:1], None, ALU.mult).then_inc(tile_set, 1)
                cut(1)
                out_of_turn(turn_no(b, MIX), G_MIX)
                cut(2)
                take_root(root_no(b, R_LORA), 1, 2)
                dve.tensor_scalar(tile[:, 0:QRANK], lora[:, 0:QRANK], rinv[:, 1:2], None, ALU.mult)
                dve.tensor_scalar(tile[:, QRANK:QRANK + KVRANK], lora[:, QRANK:QRANK + KVRANK], rinv[:, 2:3], None,
                                  ALU.mult).then_inc(tile_set, 1)
                kr = lora[:, QRANK + KVRANK:].unsqueeze(1).to_broadcast([P, HEADS, ROPE])
                dve.tensor_copy(qk[:, HEADS:, NOPE:], kr)
                cut(3)
                multiplied(dve, b, C_CONV + 3)
                dve.wait_ge(in_out, b * 4 + 3)
                dve.tensor_tensor(z, gate_c, pM[:, HALFC:], ALU.mult).then_inc(z_set, 1)
                dve.drain()
                dve.tensor_tensor(taps, convw[:], z.unsqueeze(1).to_broadcast([P, TAPS, CONV]), ALU.mult)\
                    .then_inc(taps_set, 1)
                cut(4)
                out_of_turn(turn_no(b, LORA), G_Q, QT + KVT)
                cut(5)
                multiplied(dve, b, C_UKV)
                kv = pS[:].rearrange("p (h d) -> p h d", h=HEADS)
                dst = vals[:, bass.ds(b, 1), :].rearrange("p b (h d) -> p (b h) d", h=HEADS)
                dve.tensor_copy(dst, kv[:, :, NOPE:]).then_inc(v_out, 1)
                dve.wait_ge(q_out, b + 1)
                dve.wait_ge(kv_out, b + 1)
                t1, t2 = qk[:, :, NOPE:NOPE + HALF], qk[:, :, NOPE + HALF:]
                cos = cos_t[:, bass.ds(b, 1), :].to_broadcast([P, 2 * HEADS, HALF])
                sin = sin_t[:, bass.ds(b, 1), :].to_broadcast([P, 2 * HEADS, HALF])
                dve.tensor_tensor(rtmp[:, 0], t1, sin, ALU.mult)
                dve.tensor_tensor(rtmp[:, 1], t2, sin, ALU.mult)
                dve.drain()
                dve.tensor_tensor(t1, t1, cos, ALU.mult)
                dve.tensor_tensor(t2, t2, cos, ALU.mult)
                dve.drain()
                dve.tensor_tensor(t1, t1, rtmp[:, 1], ALU.subtract)
                dve.tensor_tensor(t2, t2, rtmp[:, 0], ALU.add).then_inc(qk_set, 1)
                cut(6)
                dve.wait_ge(conv_set, b + 1)
                dve.wait_ge(in_out, b * 4 + 4)
                dve.tensor_tensor(tile[:, CONV:], gate_b, pM[:, 0:CONV], ALU.mult).then_inc(conv_out, 1)
                dve.wait_ge(qk_turn, b * 2 + 2)
                dve.tensor_copy(kT[:, :, bass.ds(b * P, P)], pS3[0:QK, :, :]).then_inc(kT_set, 1)
                dve.wait_ge(tail_set, b + 1)

                def mask(hd):
                    dve.wait_ge(score_set, b * HEADS + hd + 1)
                    if hd == 0:
                        dve.sem_inc(dve_past, 1)
                    if hd >= 2:
                        dve.wait_ge(prob_turn, b * HEADS + hd - 1)
                    n = keys * P
                    dve.tensor_tensor(big[:, hd % 2, 0:n], pS[:, 0:n], tri[:, bass.ds((BLOCKS - 1 - b) * P, n)], ALU.add)
                    dve.drain()
                    dve.tensor_reduce(mx[:, hd:hd + 1], big[:, hd % 2, 0:n], AX_X, ALU.max)
                    dve.drain()
                    dve.tensor_scalar(nmx[:, hd:hd + 1], mx[:, hd:hd + 1], -1.0 / math.sqrt(QK), None, ALU.mult)\
                        .then_inc(masked_set, 1)

                for c, its in enumerate(HEAD_TURNS):
                    cut(7 + c)
                    for it in its:
                        if it < HEADS:
                            mask(it)
                cut(AFTER)
                dve.wait_ge(head_out, b * HEADS + HEADS)
                dve.reciprocal(rinv[:, 32:32 + HEADS], rsum[:])
                dve.drain()
                dve.tensor_tensor(tile[:, 0:HEADS * VDIM].rearrange("p (h d) -> p h d", h=HEADS),
                                  pM[:, 0:HEADS * VDIM].rearrange("p (h d) -> p h d", h=HEADS),
                                  rinv[:, 32:32 + HEADS].unsqueeze(2).to_broadcast([P, HEADS, VDIM]), ALU.mult)
                dve.drain()
                dve.tensor_tensor(big[:, 0, :], tile[:], tile[:], ALU.mult)
                dve.drain()
                dve.tensor_reduce(ss[:, 8:8 + GROUPS], big[:, 0, :].rearrange("p (g d) -> p g d", g=GROUPS), AX_X,
                                  ALU.add).then_inc(gsum_set, 1)
                take_root(root_no(b, R_GROUP), 8, GROUPS)
                tile3 = tile[:].rearrange("p (g d) -> p g d", g=GROUPS)
                dve.tensor_tensor(tile3, tile3, rinv[:, 8:8 + GROUPS].unsqueeze(2).to_broadcast([P, GROUPS, GDIM]),
                                  ALU.mult).then_inc(tile_set, 1)
                cut(AFTER + 1)
                out_of_turn(turn_no(b, MIXED), G_OUT)
                cut(AFTER + 2)
                for half in range(2):
                    cols = slice(half * HALFC, (half + 1) * HALFC)
                    multiplied(dve, b, C_O + 2 * half + 1)
                    dve.tensor_tensor(h[:, cols], h[:, cols], pM[:, cols], ALU.add).then_inc(h_mix, 1)
                take_root(root_no(b, R_CROSS), 3)
                dve.tensor_scalar(tile[:], h[:], rinv[:, 3:4], None, ALU.mult).then_inc(tile_set, 1)
                cut(AFTER + 3)
                out_of_turn(turn_no(b, CROSS), G_X)
                cut(AFTER + 4)
                multiplied(dve, b, C_A + 3)
                dve.tensor_reduce(mx[:, 0:XHEADS], pM[:].rearrange("p (h m) -> p h m", h=XHEADS), AX_X, ALU.max)
                dve.drain()
                dve.tensor_scalar(nmx[:, 0:XHEADS], mx[:, 0:XHEADS], -1.0 / math.sqrt(XDIM), None, ALU.mult)\
                    .then_inc(xmax_set, 1)
                dve.wait_ge(xexp_set, b + 1)
                dve.reciprocal(rinv[:, 32:32 + XHEADS], rsum[:, 0:XHEADS])
                dve.drain()
                tile4 = tile[:].rearrange("p (h m) -> p h m", h=XHEADS)
                dve.tensor_tensor(tile4, tile4, rinv[:, 32:32 + XHEADS].unsqueeze(2).to_broadcast([P, XHEADS, MEM]),
                                  ALU.mult).then_inc(tile_set, 1)
                cut(AFTER + 5)
                out_of_turn(turn_no(b, PROBS), None)
                cut(AFTER + 6)
                for half in range(2):
                    cols = slice(half * HALFC, (half + 1) * HALFC)
                    multiplied(dve, b, C_B + 2 * half + 1)
                    dve.tensor_tensor(h[:, cols], h[:, cols], pM[:, cols], ALU.add).then_inc(h_cross, 1)
                take_root(root_no(b, R_FFN), 4)
                dve.scalar_tensor_tensor(out=tile[:], in0=h[:], scalar=rinv[:, 4:5], in1=g_ffn[:], op0=ALU.mult,
                                         op1=ALU.mult).then_inc(tile_set, 1)
                cut(AFTER + 7)
                out_of_turn(turn_no(b, FFN), None)
                cut(AFTER + 8)
                cut(AFTER + 9)
                out_of_turn(turn_no(b, PEERQ), None)
                cut(TOPK_AT)
                dve.wait_ge(pscore_out, b + 1)
                dve.sem_inc(dve_past, 1)
                for part in range(4):
                    if part:
                        cut(TOPK_AT + part)
                    sets = range(4 * part, 4 * part + 4)
                    for s in sets:
                        dve.max(best_v[:, s, 0:8], pscore[:, s, :])
                    dve.drain()
                    for s in sets:
                        dve.max_index(best_i[:, s, 0:8], best_v[:, s, 0:8], pscore[:, s, :])
                        dve.match_replace(rest[:, s % 8, :], best_v[:, s, 0:8], pscore[:, s, :], LOWEST)
                    dve.drain()
                    for s in sets:
                        dve.max(best_v[:, s, 8:16], rest[:, s % 8, :])
                    dve.drain()
                    for s in sets:
                        dve.max_index(best_i[:, s, 8:16], best_v[:, s, 8:16], rest[:, s % 8, :])
                cut(TOPK_AT + 4)
                dve.drain()
                dve.tensor_copy(best_f[:], best_i[:])
                dve.drain()
                f4 = best_f[:].rearrange("p (c h) k -> p h c k", h=PHEADS)
                v4 = best_v[:].rearrange("p (c h) k -> p h c k", h=PHEADS)
                dve.tensor_scalar(f4[:, :, 0, :], f4[:, :, 0, :], float(PKEYS), None, ALU.mult)
                dve.drain()
                at = 0
                for i0, ni, nj in RECTS:
                    for src, dst in ((v4, cand_v), (f4, cand_i)):
                        a = src[:, :, 0, i0:i0 + ni].unsqueeze(3).to_broadcast([P, PHEADS, ni, nj])
                        c = src[:, :, 1, 0:nj].unsqueeze(2).to_broadcast([P, PHEADS, ni, nj])
                        d = dst[:, :, at:at + ni * nj].rearrange("p h (i j) -> p h i j", i=ni)
                        dve.tensor_tensor(d, a, c, ALU.add)
                    at += ni * nj
                dve.drain()
                for hd in range(PHEADS):
                    dve.max(top_v[:, hd, 0:8], cand_v[:, hd, :])
                dve.drain()
                for hd in range(PHEADS):
                    dve.max_index(top_p[:, hd, 0:8], top_v[:, hd, 0:8], cand_v[:, hd, :])
                    dve.match_replace(cand_r[:, hd, :], top_v[:, hd, 0:8], cand_v[:, hd, :], LOWEST)
                dve.drain()
                for hd in range(PHEADS):
                    dve.max(top_v[:, hd, 8:16], cand_r[:, hd, :])
                dve.drain()
                for hd in range(PHEADS):
                    dve.max_index(top_p[:, hd, 8:16], top_v[:, hd, 8:16], cand_r[:, hd, :])
                dve.drain()
                dve.tensor_copy(top_f, top_p)
                dve.drain()
                chosen_f = best_f[:].rearrange("p s k -> p (s k)")[:, 0:EXPERTS]
                for c, heads in enumerate(((0, 1, 2), (3, 4, 5), (6, 7))):
                    cut(TOPK_AT + 5 + c)
                    for hd in heads:
                        t = hit[hd % 2]
                        dve.tensor_tensor(t, iota_c[:].unsqueeze(1).to_broadcast([P, TOPK, CAND]),
                                          top_f[:, hd, :].unsqueeze(2).to_broadcast([P, TOPK, CAND]), ALU.is_equal)
                        dve.drain()
                        dve.tensor_tensor(t, t, cand_i[:, hd, :].unsqueeze(1).to_broadcast([P, TOPK, CAND]), ALU.mult)
                        dve.drain()
                        dve.tensor_reduce(chosen_f[:, hd * TOPK:(hd + 1) * TOPK], t, AX_X, ALU.add)
                dve.drain()
                if keys > 1:
                    dve.wait_ge(idx_taken, b)
                    dve.wait_ge(gates_taken, b)
                dve.tensor_copy(idx_next[:], chosen_f)
                dve.tensor_tensor(top_m, top_v, top_v[:, :, 0:1].to_broadcast([P, PHEADS, TOPK]), ALU.subtract)\
                    .then_inc(gate_in, 1)
                dve.wait_ge(gate_exp, b + 1)
                dve.tensor_reduce(mx[:], top_f, AX_X, ALU.add)
                dve.drain()
                dve.reciprocal(rinv[:, 32:32 + PHEADS], mx[:])
                dve.drain()
                dve.tensor_tensor(gates_next[:].rearrange("p (h k) -> p h k", h=PHEADS), top_f,
                                  rinv[:, 32:32 + PHEADS].unsqueeze(2).to_broadcast([P, PHEADS, TOPK]), ALU.mult)\
                    .then_inc(chosen, 1)
                for c in range(CHOSEN_AT + 1, CUTS):
                    cut(c)

            def stage(b):
                dve.wait_ge(ring_open, b * EXPERTS + EXPERTS + RING)
                dve.tensor_copy(out_stage, acc[:]).then_inc(acc_out, 1)

            def finish(b):
                dve.wait_ge(final_root, b + 1)
                dve.reciprocal(rinv[:, 5:6], std[:, 5:6])
                dve.drain()
                dve.scalar_tensor_tensor(out=out_stage, in0=out_stage, scalar=rinv[:, 5:6], in1=g_fin[:], op0=ALU.mult,
                                         op1=ALU.mult).then_inc(out_set, 1)

            def boundary():
                dve.drain()
                dve.tensor_copy(hn[:], tile[:]).then_inc(hn_taken, 1)
                dve.drain()

            dve.memset(eps[:], EPS).then_inc(dve_set, 1)
            dve.wait_ge(consts_in, 48)
            dve.tensor_copy(posf, posi)
            dve.drain()
            a = [ang[:, k] for k in range(4)]
            dve.tensor_tensor(a[0], posf.unsqueeze(2).to_broadcast([P, BLOCKS, HALF]),
                              invf.unsqueeze(1).to_broadcast([P, BLOCKS, HALF]), ALU.mult)
            dve.drain()
            dve.tensor_scalar(a[1], a[0], 1.0 / (2 * math.pi), ROUNDER, ALU.mult, ALU.add)
            dve.drain()
            dve.tensor_scalar(a[1], a[1], ROUNDER, None, ALU.subtract)
            dve.drain()
            for part in TURN_PARTS:
                dve.scalar_tensor_tensor(out=a[0], in0=a[1], scalar=-part, in1=a[0], op0=ALU.mult, op1=ALU.add)
                dve.drain()
            dve.tensor_scalar(a[2], a[0], PI_BELOW, -PI_BELOW, ALU.min, ALU.max)
            dve.drain()
            dve.scalar_tensor_tensor(out=a[3], in0=a[2], scalar=-1.0, in1=a[2], op0=ALU.mult, op1=ALU.max)
            dve.drain()
            dve.tensor_scalar(a[3], a[3], -1.0, math.pi / 2, ALU.mult, ALU.add).then_inc(angle_set, 1)
            for m in range(2):
                take_root(m + 1, 6 + m)
                dve.tensor_scalar(tile[:], memx[:, m, :], rinv[:, 6 + m:7 + m], None, ALU.mult).then_inc(tile_set, 1)
                out_of_turn(m + 1, G_MEM, dst=memT[:, :, m * P:(m + 1) * P])
            dve.wait_ge(pool_set, POOL_CONSTS)
            dve.wait_ge(gains_in, 48)
            dve.wait_ge(sincos_set, 1)

            front(0, 1, lambda c: None)
            boundary()
            for first, last in LOOPS:
                with dve.Fori(first, last) as b:
                    front(b, last, lambda c: steps(b - 1, c // 2, c % 2))
                    stage(b - 1)
                    boundary()
                    finish(b - 1)
            with dve.Fori(0, CUTS // 2) as r:
                for par in range(2):
                    steps(BLOCKS - 1, r, par)
            dve.wait_ge(out_stored, 16 * (BLOCKS - 1))
            stage(BLOCKS - 1)
            finish(BLOCKS - 1)


def _chunks(m, halves, cols):
    return m.reshape(2, 4, P, halves, cols).transpose(3, 0, 2, 1, 4).reshape(2 * halves, P, 4 * cols)


def kernel(**inputs):
    import numpy as np
    import concourse.bacc as bacc
    from concourse.bass_utils import run_bass_kernel_spmd as run

    g = {k: np.asarray(v) for k, v in inputs.items()}
    one = {k: v[0] for k, v in g.items() if k != "g_final"}
    w_in = one["w_in"]
    at = np.cumsum([0, QRANK, KVRANK + ROPE, CONV, CONV, CONV])
    gate_b, gate_c, hx = (w_in[:, at[i]:at[i + 1]] for i in (2, 3, 4))
    arrays = {
        "x": one["x"], "mem": one["mem"],
        "pos": one["positions"].reshape(BLOCKS, P).T,
        "inv_freq": (np.float32(10000.0) ** (-np.arange(0, ROPE, 2, dtype=np.float32) / np.float32(ROPE)))[None],
        "gcol": np.concatenate([one[k].reshape(-1, P).T for k in ("g_mix", "g_q", "g_kv", "g_out", "g_x", "g_mem")], 1),
        "g_ffn": one["g_ffn"][None], "g_final": g["g_final"][None],
        "conv_w": one["conv_w"].reshape(1, TAPS * CONV),
        "w_cq": _chunks(w_in[:, at[0]:at[1]], 1, QRANK),
        "w_ckvr": _chunks(w_in[:, at[1]:at[2]], 1, KVRANK + ROPE),
        "w_conv": np.concatenate([_chunks(m, 1, CONV) for m in (gate_c, hx, gate_b)]),
        "w_uq": one["w_uq"].reshape(QT, P, 2, QRANK).transpose(2, 1, 0, 3).reshape(2, P, QT * QRANK),
        "w_ukv": one["w_ukv"].reshape(KVT, P, D).transpose(1, 0, 2).reshape(1, P, KVT * D),
        "w_o": _chunks(one["w_o"], 2, HALFC),
        "w_pq": _chunks(one["w_pq"], 2, HALFC),
        "keys": one["sub_keys"].transpose(1, 3, 0, 2).reshape(1, P, PHEADS * PKEYS),
        "w_xkv": _chunks(one["w_xkv"], 4, HALFC),
        "w_xqT": one["w_xq"].T.reshape(XHEADS, 2, P, D).transpose(0, 2, 1, 3).reshape(XHEADS, P, 2 * D),
        "w_xo": one["w_xo"].reshape(XHEADS, 2, P, D).transpose(0, 2, 1, 3).reshape(XHEADS, P, 2 * D),
        "experts": np.concatenate([one["u_experts"], one["v_experts"]], axis=1),
    }
    arrays = {k: np.ascontiguousarray(v) for k, v in arrays.items()}
    nc = bacc.Bacc("TRN2", target_bir_lowering=False, num_devices=1)
    w = {k: nc.dram_tensor("in_" + k, a.shape, mybir.dt.from_np(a.dtype), kind="ExternalInput").ap() for k, a in arrays.items()}
    for name in ("cross_a", "cross_b"):
        w[name] = nc.dram_tensor(name, [4, P, WCHUNK], F32, kind="Internal").ap()
    out = nc.dram_tensor("out", [1, SEQ, D], F32, kind="ExternalOutput").ap()
    layer_kernel(nc, w, out[0])
    return run(nc, [{"in_" + k: a for k, a in arrays.items()}], core_ids=[0]).results[0]["out"]
```
